# Optimizing a Trainium2 kernel written in Bass

```python
import jax, jax.numpy as jnp
from jax import lax
import numpy as np

D_MODEL = 1024
BATCH = 1
SEQ = 256
DEPTH = 1

GRID_W = 64
N_MEM = 256
EPS = 1e-6

ATT_HEADS = 8
ATT_KV_HEADS = 2
ATT_HEAD_DIM = 64
ATT_WIDTH = ATT_HEADS * ATT_HEAD_DIM
KV_WIDTH = ATT_KV_HEADS * ATT_HEAD_DIM
ROPE_THETA = 10000.0
Q_BLOCK = 128

SGU_GROUPS = 4
SGU_WIDTH = 512
SGU_GROUP_CH = SGU_WIDTH // SGU_GROUPS
SGU_CHUNK = 128

IN_COLS = ATT_WIDTH + 2 * KV_WIDTH + 2 * SGU_WIDTH + 2 * D_MODEL

X_HEADS = 4
X_HEAD_DIM = 128
X_WIDTH = X_HEADS * X_HEAD_DIM

N_GROUPS = 4
EXPERTS_PER_GROUP = 4
N_EXPERTS = N_GROUPS * EXPERTS_PER_GROUP
TOP_K = 2
D_EXPERT = 512


def rms_norm(x, g):
    xf = x.astype(jnp.float32)
    y = xf * lax.rsqrt(jnp.mean(xf * xf, axis=-1, keepdims=True) + EPS)
    return y.astype(x.dtype) * g

def layer_norm(x, g, b):
    xf = x.astype(jnp.float32)
    mu = jnp.mean(xf, axis=-1, keepdims=True)
    xc = xf - mu
    var = jnp.mean(xc * xc, axis=-1, keepdims=True)
    return (xc * lax.rsqrt(var + EPS)).astype(x.dtype) * g + b

def axial_rope_tables(seq_len):
    rows = seq_len // GRID_W
    row_ids = jnp.repeat(jnp.arange(rows), GRID_W).astype(jnp.float32)
    col_ids = jnp.tile(jnp.arange(GRID_W), rows).astype(jnp.float32)
    pairs_per_axis = ATT_HEAD_DIM // 4
    inv_freq = ROPE_THETA ** (-jnp.arange(pairs_per_axis, dtype=jnp.float32) / pairs_per_axis)
    ang = jnp.concatenate([row_ids[:, None] * inv_freq[None, :],
                           col_ids[:, None] * inv_freq[None, :]], axis=-1)
    return jnp.cos(ang), jnp.sin(ang)

def apply_rope(x, cos, sin):
    xf = x.astype(jnp.float32).reshape(*x.shape[:-1], x.shape[-1] // 2, 2)
    x0, x1 = xf[..., 0], xf[..., 1]
    c = cos[None, :, None, :]
    s = sin[None, :, None, :]
    out = jnp.stack([x0 * c - x1 * s, x0 * s + x1 * c], axis=-1).reshape(x.shape)
    return out.astype(x.dtype)

def gqa_attention(q, k, v):
    B, S, _, HD = q.shape
    G = ATT_HEADS // ATT_KV_HEADS
    nb = S // Q_BLOCK
    qb = q.reshape(B, nb, Q_BLOCK, ATT_KV_HEADS, G, HD).transpose(1, 0, 2, 3, 4, 5)
    scale = HD ** -0.5

    def block(q_blk):
        s = jnp.einsum('bqhgd,bkhd->bhgqk', q_blk, k, preferred_element_type=jnp.float32) * scale
        p = jax.nn.softmax(s, axis=-1).astype(v.dtype)
        return jnp.einsum('bhgqk,bkhd->bqhgd', p, v)

    o = lax.map(block, qb)
    return o.transpose(1, 0, 2, 3, 4, 5).reshape(B, S, ATT_WIDTH)

def spatial_gating(u, v, w_s, b_s, ln_g, ln_b):
    B, S, _ = v.shape
    nc = S // SGU_CHUNK
    vn = layer_norm(v, ln_g, ln_b).reshape(B, nc, SGU_CHUNK, SGU_GROUPS, SGU_GROUP_CH)
    vm = jnp.einsum('gpq,bnqgc->bnpgc', w_s, vn) + b_s.T[:, :, None]
    return u * vm.reshape(B, S, SGU_WIDTH)

def memory_cross_attention(h, mem_n, w_cq, w_ckv, w_co):
    B, S, _ = h.shape
    M = mem_n.shape[1]
    q = (h @ w_cq).reshape(B, S, X_HEADS, X_HEAD_DIM)
    kv = mem_n @ w_ckv
    k = kv[..., :X_WIDTH].reshape(B, M, X_HEADS, X_HEAD_DIM)
    v = kv[..., X_WIDTH:].reshape(B, M, X_HEADS, X_HEAD_DIM)
    s = jnp.einsum('bshd,bmhd->bhsm', q, k, preferred_element_type=jnp.float32) * (X_HEAD_DIM ** -0.5)
    p = jax.nn.softmax(s, axis=-1).astype(v.dtype)
    o = jnp.einsum('bhsm,bmhd->bshd', p, v).reshape(B, S, X_WIDTH)
    return o @ w_co

def hierarchical_moe(h, w_rg, b_rg, w_re, b_re, w_gate, w_up, w_down):
    B, S, D = h.shape
    t = h.reshape(B * S, D)
    glog = (t @ w_rg + b_rg).astype(jnp.float32)
    gprob = jax.nn.softmax(glog, axis=-1)
    gval, gidx = lax.top_k(gprob, 1)
    elog = (t @ w_re + b_re).astype(jnp.float32).reshape(-1, N_GROUPS, EXPERTS_PER_GROUP)
    elog_sel = jnp.take_along_axis(elog, gidx[:, :, None], axis=1)[:, 0]
    evals, eidx = lax.top_k(elog_sel, TOP_K)
    ew = jax.nn.softmax(evals, axis=-1) * gval
    expert_id = gidx * EXPERTS_PER_GROUP + eidx
    combine = jnp.sum(jax.nn.one_hot(expert_id, N_EXPERTS, dtype=jnp.float32) * ew[..., None], axis=1)
    combine = combine.astype(t.dtype)
    y = jnp.zeros_like(t)
    for e in range(N_EXPERTS):
        he = jax.nn.silu(t @ w_gate[e]) * (t @ w_up[e])
        y = y + combine[:, e:e + 1] * (he @ w_down[e])
    return y.reshape(B, S, D)

def first_inputs(seed: int = 0) -> dict:
    key = jax.random.key(seed)
    ks = iter(jax.random.split(key, 40))
    L = DEPTH
    f32 = jnp.float32

    def nrm(shape, scale):
        return jax.random.normal(next(ks), shape, f32) * scale

    def gain(shape):
        return 1.0 + 0.1 * jax.random.normal(next(ks), shape, f32)

    return {
        'x': nrm((BATCH, SEQ, D_MODEL), 1.0),
        'mem': nrm((BATCH, N_MEM, D_MODEL), 1.0),
        'g_mix': gain((L, D_MODEL)),
        'w_in': nrm((L, D_MODEL, IN_COLS), D_MODEL ** -0.5),
        'g_q': gain((L, ATT_HEAD_DIM)),
        'g_k': gain((L, ATT_HEAD_DIM)),
        'w_att_out': nrm((L, ATT_WIDTH, D_MODEL), ATT_WIDTH ** -0.5),
        'sgu_ln_g': gain((L, SGU_WIDTH)),
        'sgu_ln_b': nrm((L, SGU_WIDTH), 0.02),
        'w_s': nrm((L, SGU_GROUPS, SGU_CHUNK, SGU_CHUNK), 0.5 * SGU_CHUNK ** -0.5),
        'b_s': 1.0 + nrm((L, SGU_GROUPS, SGU_CHUNK), 0.1),
        'w_sgu_out': nrm((L, SGU_WIDTH, D_MODEL), SGU_WIDTH ** -0.5),
        'w_out': nrm((L, D_MODEL, D_MODEL), D_MODEL ** -0.5),
        'g_cross': gain((L, D_MODEL)),
        'g_mem': gain((L, D_MODEL)),
        'w_cq': nrm((L, D_MODEL, X_WIDTH), D_MODEL ** -0.5),
        'w_ckv': nrm((L, D_MODEL, 2 * X_WIDTH), D_MODEL ** -0.5),
        'w_co': nrm((L, X_WIDTH, D_MODEL), X_WIDTH ** -0.5),
        'g_moe': gain((L, D_MODEL)),
        'w_rg': nrm((L, D_MODEL, N_GROUPS), D_MODEL ** -0.5),
        'b_rg': nrm((L, N_GROUPS), 0.01),
        'w_re': nrm((L, D_MODEL, N_EXPERTS), D_MODEL ** -0.5),
        'b_re': nrm((L, N_EXPERTS), 0.01),
        'w_gate': nrm((L, N_EXPERTS, D_MODEL, D_EXPERT), D_MODEL ** -0.5),
        'w_up': nrm((L, N_EXPERTS, D_MODEL, D_EXPERT), D_MODEL ** -0.5),
        'w_down': nrm((L, N_EXPERTS, D_EXPERT, D_MODEL), D_EXPERT ** -0.5),
        'g_final': gain((D_MODEL,)),
    }

def first_block(x, mem, g_mix, w_in, g_q, g_k, w_att_out, sgu_ln_g, sgu_ln_b, w_s, b_s,
              w_sgu_out, w_out, g_cross, g_mem, w_cq, w_ckv, w_co, g_moe, w_rg, b_rg,
              w_re, b_re, w_gate, w_up, w_down, g_final):
    B, S, _ = x.shape
    cos, sin = axial_rope_tables(S)
    splits = [ATT_WIDTH,
              ATT_WIDTH + KV_WIDTH,
              ATT_WIDTH + 2 * KV_WIDTH,
              ATT_WIDTH + 2 * KV_WIDTH + SGU_WIDTH,
              ATT_WIDTH + 2 * KV_WIDTH + 2 * SGU_WIDTH,
              ATT_WIDTH + 2 * KV_WIDTH + 2 * SGU_WIDTH + D_MODEL]
    for l in range(DEPTH):
        h = rms_norm(x, g_mix[l])
        z = h @ w_in[l]
        q, k, v, su, sv, ga, gb = jnp.split(z, splits, axis=-1)
        q = rms_norm(q.reshape(B, S, ATT_HEADS, ATT_HEAD_DIM), g_q[l])
        k = rms_norm(k.reshape(B, S, ATT_KV_HEADS, ATT_HEAD_DIM), g_k[l])
        q = apply_rope(q, cos, sin)
        k = apply_rope(k, cos, sin)
        v = v.reshape(B, S, ATT_KV_HEADS, ATT_HEAD_DIM)
        y_att = gqa_attention(q, k, v) @ w_att_out[l]
        y_sgu = spatial_gating(jax.nn.gelu(su), jax.nn.gelu(sv), w_s[l], b_s[l],
                               sgu_ln_g[l], sgu_ln_b[l]) @ w_sgu_out[l]
        merged = jax.nn.sigmoid(ga) * y_att + jax.nn.sigmoid(gb) * y_sgu
        x = x + merged @ w_out[l]
        x = x + memory_cross_attention(rms_norm(x, g_cross[l]), rms_norm(mem, g_mem[l]),
                                       w_cq[l], w_ckv[l], w_co[l])
        x = x + hierarchical_moe(rms_norm(x, g_moe[l]), w_rg[l], b_rg[l], w_re[l], b_re[l],
                                 w_gate[l], w_up[l], w_down[l])
    return rms_norm(x, g_final)


DEPTH_2 = 2

N_MIXERS = 2
SB_HEADS = 16
SB_HEAD_DIM = D_MODEL // SB_HEADS
RET_HEADS = 8
RET_QK_DIM = D_MODEL // RET_HEADS
RET_V_DIM = 2 * RET_QK_DIM
RET_CHUNK = 128
ROPE_BASE = 10000.0
N_EXPERTS_2 = 16
EXPERTS_PER_GROUP_2 = N_EXPERTS_2 // N_GROUPS
D_EXPERT_2 = D_MODEL // 2
N_SB = (DEPTH_2 + 1) // 2
N_RET = DEPTH_2 // 2
DEEPNORM_ALPHA = (2 * DEPTH_2) ** 0.25
DEEPNORM_BETA = (8 * DEPTH_2) ** -0.25
LN_EPS = 1e-5


def layer_norm_2(x, g, b):
    xf = x.astype(jnp.float32)
    mu = jnp.mean(xf, axis=-1, keepdims=True)
    var = jnp.mean(jnp.square(xf - mu), axis=-1, keepdims=True)
    y = (xf - mu) * lax.rsqrt(var + LN_EPS) * g.astype(jnp.float32) + b.astype(jnp.float32)
    return y.astype(x.dtype)

def adaln_params(c, w, b):
    m = jax.nn.silu(c) @ w + b
    shift, scale, gate = jnp.split(m, 3, axis=-1)
    return shift[:, None, :], scale[:, None, :], gate[:, None, :]

def stick_breaking_attention(h, w_in, w_out):
    B, S, _ = h.shape
    qkv = (h @ w_in).reshape(B, S, 3, SB_HEADS, SB_HEAD_DIM)
    q = qkv[:, :, 0].transpose(0, 2, 1, 3)
    k = qkv[:, :, 1].transpose(0, 2, 1, 3)
    v = qkv[:, :, 2].transpose(0, 2, 1, 3)
    n_blocks = S // Q_BLOCK
    q_blocks = q.reshape(B, SB_HEADS, n_blocks, Q_BLOCK, SB_HEAD_DIM).transpose(2, 0, 1, 3, 4)
    key_pos = jnp.arange(S)
    scale = SB_HEAD_DIM ** -0.5

    def block(args):
        qb, i = args
        z = jnp.einsum('bhqd,bhkd->bhqk', qb, k).astype(jnp.float32) * scale
        q_pos = i * Q_BLOCK + jnp.arange(Q_BLOCK)
        causal = key_pos[None, :] < q_pos[:, None]
        log_keep = jnp.where(causal, jax.nn.log_sigmoid(-z), 0.0)
        suffix = lax.cumsum(log_keep, axis=3, reverse=True) - log_keep
        a = jnp.where(causal, jnp.exp(jax.nn.log_sigmoid(z) + suffix), 0.0)
        return jnp.einsum('bhqk,bhkd->bhqd', a.astype(v.dtype), v)

    o = lax.map(block, (q_blocks, jnp.arange(n_blocks)))
    o = o.transpose(1, 0, 3, 2, 4).reshape(B, S, D_MODEL)
    return o @ w_out

def rotary(x, cos, sin):
    half = x.shape[-1] // 2
    x1, x2 = x[..., :half], x[..., half:]
    return jnp.concatenate([x1 * cos - x2 * sin, x2 * cos + x1 * sin], axis=-1)

def retention(h, positions, w_in, gn_g, w_out):
    B, S, _ = h.shape
    f32 = jnp.float32
    proj = h @ w_in
    q, k, v, g = jnp.split(proj, [D_MODEL, 2 * D_MODEL, 4 * D_MODEL], axis=-1)
    q = q.reshape(B, S, RET_HEADS, RET_QK_DIM).astype(f32)
    k = k.reshape(B, S, RET_HEADS, RET_QK_DIM).astype(f32) * (RET_QK_DIM ** -0.5)
    v = v.reshape(B, S, RET_HEADS, RET_V_DIM).astype(f32)
    inv_freq = 1.0 / (ROPE_BASE ** (jnp.arange(0, RET_QK_DIM, 2, dtype=f32) / RET_QK_DIM))
    ang = positions.astype(f32)[..., None] * inv_freq
    cos = jnp.cos(ang)[:, :, None, :]
    sin = jnp.sin(ang)[:, :, None, :]
    q = rotary(q, cos, sin)
    k = rotary(k, cos, sin)

    log_gamma = jnp.log(1.0 - jnp.exp2(-5.0 - jnp.arange(RET_HEADS, dtype=f32)))
    n = jnp.arange(RET_CHUNK, dtype=f32)
    diff = n[:, None] - n[None, :]
    dmask = jnp.where(diff >= 0, jnp.exp(jnp.maximum(diff, 0.0) * log_gamma[:, None, None]), 0.0)
    xi = jnp.exp((n + 1.0) * log_gamma[:, None])
    zeta = jnp.exp((RET_CHUNK - 1.0 - n) * log_gamma[:, None])
    chunk_decay = jnp.exp(RET_CHUNK * log_gamma)
    n_chunks = S // RET_CHUNK

    def chunks(t):
        return t.reshape(B, n_chunks, RET_CHUNK, RET_HEADS, t.shape[-1]).transpose(1, 0, 3, 2, 4)

    def step(state, xs):
        qc, kc, vc = xs
        qk = jnp.einsum('bhnd,bhmd->bhnm', qc, kc) * dmask
        inner = jnp.einsum('bhnm,bhme->bhne', qk, vc)
        cross = jnp.einsum('bhnd,bhde->bhne', qc, state) * xi[None, :, :, None]
        state = state * chunk_decay[None, :, None, None] + jnp.einsum(
            'bhmd,bhme->bhde', kc * zeta[None, :, :, None], vc)
        return state, inner + cross

    state0 = jnp.zeros((B, RET_HEADS, RET_QK_DIM, RET_V_DIM), f32)
    _, o = lax.scan(step, state0, (chunks(q), chunks(k), chunks(v)))
    o = o.transpose(1, 0, 3, 2, 4).reshape(B, S, RET_HEADS, RET_V_DIM)
    mu = jnp.mean(o, axis=-1, keepdims=True)
    var = jnp.mean(jnp.square(o - mu), axis=-1, keepdims=True)
    o = ((o - mu) * lax.rsqrt(var + LN_EPS)).reshape(B, S, 2 * D_MODEL) * gn_g.astype(f32)
    return (jax.nn.silu(g) * o.astype(h.dtype)) @ w_out

def grouped_moe(h, router_w, router_b, w_gate, w_up, w_down):
    B, S, Dm = h.shape
    t = h.reshape(B * S, Dm)
    logits = t.astype(jnp.float32) @ router_w.astype(jnp.float32) + router_b.astype(jnp.float32)
    probs = jax.nn.softmax(logits, axis=-1)
    grouped = probs.reshape(-1, N_GROUPS, EXPERTS_PER_GROUP_2)
    group_score = jnp.sum(lax.top_k(grouped, TOP_K)[0], axis=-1)
    sel_group = jnp.argmax(group_score, axis=-1)
    expert_group = jnp.arange(N_EXPERTS_2) // EXPERTS_PER_GROUP_2
    in_group = expert_group[None, :] == sel_group[:, None]
    masked = jnp.where(in_group, logits, -jnp.inf)
    top_val, top_idx = lax.top_k(masked, TOP_K)
    top_w = jax.nn.softmax(top_val, axis=-1)
    combine = jnp.sum(jax.nn.one_hot(top_idx, N_EXPERTS_2, dtype=jnp.float32) * top_w[..., None], axis=1)
    out = jnp.zeros(t.shape, jnp.float32)
    for e in range(N_EXPERTS_2):
        hidden = jax.nn.silu(t @ w_gate[e]) * (t @ w_up[e])
        out = out + combine[:, e:e + 1] * (hidden @ w_down[e]).astype(jnp.float32)
    return out.astype(h.dtype).reshape(B, S, Dm)

def second_inputs(seed: int = 0) -> dict:
    key = jax.random.key(seed)
    ks = jax.random.split(key, 20)
    D, F = D_MODEL, D_EXPERT_2
    nrm = jax.random.normal
    x = nrm(ks[0], (BATCH, SEQ, D), jnp.float32)
    c = nrm(ks[1], (BATCH, D), jnp.float32)
    positions = jnp.broadcast_to(jnp.arange(SEQ, dtype=jnp.int32)[None, :], (BATCH, SEQ))
    ada_w = nrm(ks[2], (DEPTH_2, 2, D, 3 * D), jnp.float32) * (0.5 * D ** -0.5)
    ada_b = nrm(ks[3], (DEPTH_2, 2, 3 * D), jnp.float32) * 0.02
    ln_g = 1.0 + 0.02 * nrm(ks[4], (DEPTH_2, 2, D), jnp.float32)
    ln_b = 0.02 * nrm(ks[5], (DEPTH_2, 2, D), jnp.float32)
    sb_col = jnp.concatenate([jnp.ones((2 * D,), jnp.float32), jnp.full((D,), DEEPNORM_BETA, jnp.float32)])
    sb_w_in = nrm(ks[6], (N_SB, D, 3 * D), jnp.float32) * (D ** -0.5) * sb_col
    sb_w_out = nrm(ks[7], (N_SB, D, D), jnp.float32) * (D ** -0.5) * DEEPNORM_BETA
    ret_col = jnp.concatenate([jnp.ones((2 * D,), jnp.float32), jnp.full((2 * D,), DEEPNORM_BETA, jnp.float32),
                               jnp.ones((2 * D,), jnp.float32)])
    ret_w_in = nrm(ks[8], (N_RET, D, 6 * D), jnp.float32) * (D ** -0.5) * ret_col
    ret_gn_g = 1.0 + 0.02 * nrm(ks[9], (N_RET, 2 * D), jnp.float32)
    ret_w_out = nrm(ks[10], (N_RET, 2 * D, D), jnp.float32) * ((2 * D) ** -0.5) * DEEPNORM_BETA
    router_w = nrm(ks[11], (D, N_EXPERTS_2), jnp.float32) * (D ** -0.5)
    router_b = nrm(ks[12], (N_EXPERTS_2,), jnp.float32) * 0.01
    moe_w_gate = nrm(ks[13], (DEPTH_2, N_EXPERTS_2, D, F), jnp.float32) * (D ** -0.5)
    moe_w_up = nrm(ks[14], (DEPTH_2, N_EXPERTS_2, D, F), jnp.float32) * (D ** -0.5) * DEEPNORM_BETA
    moe_w_down = nrm(ks[15], (DEPTH_2, N_EXPERTS_2, F, D), jnp.float32) * (F ** -0.5) * DEEPNORM_BETA
    return {"x": x, "c": c, "positions": positions, "ada_w": ada_w, "ada_b": ada_b,
            "ln_g": ln_g, "ln_b": ln_b, "sb_w_in": sb_w_in, "sb_w_out": sb_w_out,
            "ret_w_in": ret_w_in, "ret_gn_g": ret_gn_g, "ret_w_out": ret_w_out,
            "router_w": router_w, "router_b": router_b, "moe_w_gate": moe_w_gate,
            "moe_w_up": moe_w_up, "moe_w_down": moe_w_down}

def second_block(x, c, positions, ada_w, ada_b, ln_g, ln_b, sb_w_in, sb_w_out, ret_w_in, ret_gn_g,
              ret_w_out, router_w, router_b, moe_w_gate, moe_w_up, moe_w_down):
    for i in range(DEPTH_2):
        shift, scale, gate = adaln_params(c, ada_w[i, 0], ada_b[i, 0])
        h = x * (1.0 + scale) + shift
        if i % N_MIXERS == 0:
            y = stick_breaking_attention(h, sb_w_in[i // 2], sb_w_out[i // 2])
        else:
            y = retention(h, positions, ret_w_in[i // 2], ret_gn_g[i // 2], ret_w_out[i // 2])
        x = layer_norm_2(DEEPNORM_ALPHA * x + (1.0 + gate) * y, ln_g[i, 0], ln_b[i, 0])
        shift, scale, gate = adaln_params(c, ada_w[i, 1], ada_b[i, 1])
        h = x * (1.0 + scale) + shift
        y = grouped_moe(h, router_w, router_b, moe_w_gate[i], moe_w_up[i], moe_w_down[i])
        x = layer_norm_2(DEEPNORM_ALPHA * x + (1.0 + gate) * y, ln_g[i, 1], ln_b[i, 1])
    return x


def setup_inputs(seed=0):
    out = dict(first_inputs(seed))
    for name, value in second_inputs(seed + 1).items():
        if name != "x":
            out[name + "_2"] = value
    return out


def reference(
    x, mem, g_mix, w_in, g_q, g_k, w_att_out, sgu_ln_g, sgu_ln_b, w_s, b_s, w_sgu_out, w_out,
    g_cross, g_mem, w_cq, w_ckv, w_co, g_moe, w_rg, b_rg, w_re, b_re, w_gate, w_up, w_down,
    g_final, c_2, positions_2, ada_w_2, ada_b_2, ln_g_2, ln_b_2, sb_w_in_2, sb_w_out_2,
    ret_w_in_2, ret_gn_g_2, ret_w_out_2, router_w_2, router_b_2, moe_w_gate_2, moe_w_up_2,
    moe_w_down_2,
):
    x = first_block(
        x, mem, g_mix, w_in, g_q, g_k, w_att_out, sgu_ln_g, sgu_ln_b, w_s, b_s, w_sgu_out,
        w_out, g_cross, g_mem, w_cq, w_ckv, w_co, g_moe, w_rg, b_rg, w_re, b_re, w_gate, w_up,
        w_down, g_final,
    )
    return second_block(
        x, c_2, positions_2, ada_w_2, ada_b_2, ln_g_2, ln_b_2, sb_w_in_2, sb_w_out_2,
        ret_w_in_2, ret_gn_g_2, ret_w_out_2, router_w_2, router_b_2, moe_w_gate_2, moe_w_up_2,
        moe_w_down_2,
    )


_drawn_inputs = setup_inputs


def setup_inputs(seed=0):
    import zlib

    import numpy as np

    out = dict(_drawn_inputs(seed))
    spreads = {}
    factors = {'b_rg': 2.683, 'ret_gn_g_2': 8.0, 'router_b_2': 8.0}
    for name, (base, spread) in spreads.items():
        noise = np.random.default_rng([zlib.crc32(name.encode()), seed]).standard_normal(out[name].shape)
        drawn = base * np.exp(spread * noise) if base else spread * noise
        out[name] = __import__('jax').numpy.asarray(drawn.astype(out[name].dtype))
    for name, factor in factors.items():
        out[name] = (out[name] * factor).astype(out[name].dtype)
    return out
```

```python
from contextlib import ExitStack

import concourse.bass as bass
import numpy as np
from concourse import mybir

F32 = mybir.dt.float32
I32 = mybir.dt.int32
U32 = mybir.dt.uint32
ALU = mybir.AluOpType
ACT = mybir.ActivationFunctionType
AX = mybir.AxisListType.X

P = 128
SEQ = 256
NT = SEQ // P
D = 1024
KC = D // P
PAN = 4096
RING = 6
CAP = 64
NE = 16
PER = 3
EPS_RMS = 1e-6
EPS_LN = 1e-5
ALPHA = 4.0 ** 0.25
ATT_SCALE = 64.0 ** -0.5
X_SCALE = 128.0 ** -0.5
BIG = 1e30

C_ID, C_NEGU, C_NEG1, C_CAUSAL, C_NEGMASK, C_PREFIX, C_ONES, C_SLOT = [i * P for i in range(8)]
C_ROPE = 8 * P
C_GRP = C_ROPE + 128
C_EXP = C_GRP + 16
C_OFF = C_EXP + 16
C_PICK = C_OFF + 3
C_INVF = C_PICK + 1
CST_COLS = C_INVF + 64


def constants():
    i = np.arange(P)
    c = np.zeros((P, CST_COLS), np.float32)
    c[:, C_ID:C_ID + P] = np.eye(P)
    c[:, C_NEGU:C_NEGU + P] = np.where(i[:, None] >= i[None, :], -1.0, 0.0)
    c[:, C_NEG1:C_NEG1 + P] = -1.0
    c[:, C_CAUSAL:C_CAUSAL + P] = i[:, None] < i[None, :]
    c[:, C_NEGMASK:C_NEGMASK + P] = np.where(i[:, None] < i[None, :], 0.0, -BIG)
    c[:, C_PREFIX:C_PREFIX + P] = i[:, None] < i[None, :]
    c[:, C_ONES:C_ONES + P] = 1.0
    c[:, C_SLOT:C_SLOT + P] = i[None, :] % CAP
    inv = (10000.0 ** (-np.arange(16, dtype=np.float32) / np.float32(16))).astype(np.float32)
    for t in range(NT):
        s = t * P + i
        ang = np.concatenate([(s // 64)[:, None].astype(np.float32) * inv, (s % 64)[:, None].astype(np.float32) * inv], 1)
        c[:, C_ROPE + 64 * t:C_ROPE + 64 * t + 32] = np.cos(ang)
        c[:, C_ROPE + 64 * t + 32:C_ROPE + 64 * t + 64] = np.sin(ang)
    c[:, C_GRP:C_GRP + 16] = np.arange(16) // 4
    c[:, C_EXP:C_EXP + 16] = np.arange(16)
    c[:, C_OFF:C_OFF + 3] = CAP * np.arange(1, 4)
    c[::32, C_PICK] = 1.0
    c[:, C_INVF:C_INVF + 64] = 1.0 / (np.float32(10000.0) ** (np.arange(0, 128, 2, dtype=np.float32) / np.float32(128)))
    return c


def decay_table():
    g = np.log(1.0 - np.exp2(-5.0 - np.arange(8.0)))
    m = np.arange(P)[:, None, None]
    n = np.arange(P)[None, None, :]
    lg = g[None, :, None]
    same = np.where(n >= m, np.exp(np.maximum(n - m, 0) * lg), 0.0)
    cross = np.exp((P - 1.0 - m) * lg) * np.exp((n + 1.0) * lg)
    return (np.concatenate([same, cross, same], 2) * 128.0 ** -0.5).astype(np.float32).reshape(P, 8 * 384)


def build(nc, A, out, stop, final_ready):
    ctx = ExitStack()

    def sb(name, shape, dt=F32):
        return ctx.enter_context(nc.sbuf_tensor(name, shape, dt))

    sems = {}

    def S(name):
        if name not in sems:
            sems[name] = ctx.enter_context(nc.semaphore(name))
        return sems[name]

    ring = sb("ring", [P, RING, PAN])
    X = sb("X", [P, NT, D])
    hT = sb("hT", [P, KC, SEQ])
    Z = sb("Z", [P, 12288])
    DM = sb("DM", [P, 3072])
    LNG = sb("LNG", [P, 2, D])
    GB = sb("GB", [P, D])
    CST = sb("CST", [P, CST_COLS])
    VT = sb("VT", [P, 2, 96])
    ADA = sb("ADA", [P, 96])
    AROW = sb("AROW", [P, 512])
    SILC = sb("SILC", [P, KC, 32])
    WST = sb("WST", [P, 4, P])
    WR1 = sb("WR1", [P, KC, 20])
    WR2 = sb("WR2", [P, KC, 16])
    BR1 = sb("BR1", [P, 20])
    BR2 = sb("BR2", [P, 16])
    GQK = sb("GQK", [P, 10, 64])
    SGB = GB[:, :].rearrange("p (k n) -> p k n", k=2)
    SM = sb("SM", [P, 2, 384])
    CS2 = sb("CS2", [P, 2, NT, 64])
    POS = sb("POS", [P, NT], I32)
    POSF = sb("POSF", [P, NT])
    ST = sb("ST", [P, 2, NT, 2, 6])
    MV = sb("MV", [P, 2, NT, 2])
    MS = sb("MS", [P, 2, 20])
    RS = sb("RS", [P, 2, 20])
    NEGH = sb("NEGH", [P, 20])
    SX = sb("SX", [P, 2, 3, NT])
    RTI = sb("RTI", [P, 2, NT, 8], U32)
    TBL = sb("TBL", [1, 3, 3, NE], I32)
    TBF = sb("TBF", [1, 8, NE])
    ps = ctx.enter_context(nc.psum_tensor("ps", [P, 8, 512], F32))

    def cst(at, n=P, rows=slice(0, P)):
        return CST[rows, at:at + n]

    ident = cst(C_ID)
    V_MIX, V_CROSS, V_MEM, V_MOE, V_C, V_GN, V_BS = 0, 8, 16, 24, 32, 40, 56

    filled = [S(f"filled{b}") for b in range(8)]
    drained = [S(f"drained{b}") for b in range(8)]
    uses = [0] * 8
    turn = {"A": 0, "B": 0}
    where = {}
    POOLS = {"A": [0, 1, 2, 3], "B": [4, 5, 6, 7]}

    def claim(pe, key, pool):
        b = POOLS[pool][turn[pool] % 4]
        turn[pool] += 1
        if uses[b]:
            pe.wait_ge(drained[b], uses[b])
        uses[b] += 1
        assert key not in where, key
        where[key] = (b, uses[b])
        return ps[:, b, :]

    def fill(ins, key):
        ins.then_inc(filled[where[key][0]], 1)

    def result(eng, key):
        b, k = where[key]
        eng.wait_ge(filled[b], k)
        return ps[:, b, :]

    def drain(ins, key):
        ins.then_inc(drained[where[key][0]], 1)

    def read(eng, key):
        b, k = where[key]
        eng.wait_ge(drained[b], k)

    def k8(w, c0, n=512):
        return w[:, c0:c0 + n].rearrange("(c p) n -> p c n", p=P), KC * n

    def k4(w, r0):
        return w[r0:r0 + 512, :].rearrange("(c p) n -> p c n", p=P), PAN

    ada = [A["ada_w_2"][s // 2, s % 2] for s in range(4)]
    w_in, w_ckv, sbw, rtw = A["w_in"][0], A["w_ckv"][0], A["sb_w_in_2"][0], A["ret_w_in_2"][0]
    stream = [(("ckv", j), k8(w_ckv, 512 * j)) for j in range(2)]
    IN = [("q", 0, 512), ("kv", 512, 256), ("su", 768, 512), ("sv", 1280, 512), ("ga0", 1792, 512),
          ("ga1", 2304, 512), ("gb0", 2816, 512), ("gb1", 3328, 512)]
    stream += [(("in", n), k8(w_in, c0, w)) for n, c0, w in IN]

    def ada_panels(ns):
        return [(("ada", n), k8(ada[n // 6], 512 * (n % 6))) for n in ns]

    stream += ada_panels(range(8))
    stream += [(("att_out", 0), k4(A["w_att_out"][0], 0)), (("sgu_out", 0), k4(A["w_sgu_out"][0], 0))]
    stream += [(("w_out", j), k4(A["w_out"][0], 512 * j)) for j in range(2)]
    stream += [(("cq", 0), k8(A["w_cq"][0], 0))] + ada_panels(range(8, 12)) + [(("co", 0), k4(A["w_co"][0], 0))]
    stream += [(("moe", 0), None)]
    stream += [(("sb", j), k8(sbw, 512 * j)) for j in range(6)] + ada_panels(range(12, 18))
    stream += [(("sb_out", j), k4(A["sb_w_out_2"][0], 512 * j)) for j in range(2)]
    stream += [(("moe", 1), None)]
    stream += [(("ret", j), k8(rtw, 512 * j)) for j in range(12)] + ada_panels(range(18, 24))
    stream += [(("ret_out", j), k4(A["ret_w_out_2"][0], 512 * j)) for j in range(4)]
    stream += [(("moe", 2), None)]
    MOE_W = [(A["w_gate"][0], A["w_up"][0], A["w_down"][0])] + [
        (A["moe_w_gate_2"][i], A["moe_w_up_2"][i], A["moe_w_down_2"][i]) for i in range(2)]
    if stop:
        last = max(i for i, (key, _) in enumerate(stream) if key[0] == stop[0] and (len(stop) == 1 or key[1] == stop[1]))
        stream = stream[:last + 1]
    slot_of, first_of, n = {}, {}, 0
    owner = []
    for key, src in stream:
        first_of[key] = n
        k = 1 if src else PER * NE
        owner += [(key, j) for j in range(k)]
        n += k
    dense_no, m = {}, 0
    for key, src in stream:
        if src:
            m += 1
            dense_no[key] = m
    order = [key for key, _ in stream]
    progress = [0]
    freed_by, op_reads = {}, [0]
    landed = [S(f"landed{r}") for r in range(RING)]

    def panel(pe, key, n):
        assert order[progress[0]] == key, (order[progress[0]], key)
        progress[0] += 1
        i = first_of[key]
        pe.wait_ge(landed[i % RING], 16 * (i // RING + 1))
        w = stream[order.index(key)][1][1]
        return ring[:, i % RING, 0:w].rearrange("p (c n) -> p c n", n=n)

    def zv(at, *shape):
        v = Z[:, at:at + int(np.prod(shape))]
        if len(shape) == 2:
            return v.rearrange("p (a b) -> p a b", b=shape[1])
        return v

    MEM = zv(0, NT, D)
    MEMN = zv(2048, NT, D)
    WSR = zv(4096, 512)
    VROW = zv(5248, 2, P)
    ANG, KK, RR = zv(4608, 128), zv(4736, 2, 128), zv(4992, 2, 128)
    MKT = DM[:, 0:1024].rearrange("p (h m) -> p h m", h=4)
    MVV = DM[:, 1024:2048].rearrange("p (t n) -> p t n", t=NT)
    QK5 = zv(0, NT, 640)
    SU, SV = zv(1536, NT, 512), zv(2560, NT, 512)
    GA, GBT = zv(3584, NT, D), zv(5632, NT, D)
    R5 = zv(7680, NT, 640)
    KD = zv(8960, NT, 256)
    TMP = zv(9472, 2, 512)
    GQT, GKT, GV = zv(10496, 4, SEQ), zv(11520, 2, SEQ), zv(12032, NT, P)
    QR = R5
    CQT = zv(2048, 4, SEQ)
    prob_buf = {"g": [zv(9472 + 512 * i, NT, SEQ) for i in range(2)], "c": [zv(3072 + 512 * i, NT, SEQ) for i in range(2)]}
    probT_buf = {"g": [zv(512 * i, 512) for i in range(2)], "c": [zv(4096 + 512 * i, 512) for i in range(2)]}
    SQT, SKT, SBV, SE = zv(0, 8, SEQ), zv(2048, 8, SEQ), zv(4096, NT, D), zv(6144, 16, 384)
    RV, RG = zv(0, NT, 2048), zv(4096, NT, 2048)
    RQRAW, RKRAW = zv(0, NT, D), zv(2048, NT, D)
    RQ, RK = zv(4096, NT, D), zv(6144, NT, D)
    RQT, RKT = zv(8192, 8, SEQ), zv(10240, 8, SEQ)
    RT1, RT2 = zv(10240, NT, 512), zv(11264, NT, 512)
    ROT = zv(0, 16, SEQ)

    XN = Z[:, 0:2048].rearrange("p (t d) -> p t d", t=NT)

    def mb(a, at, n):
        base = 2048 + 3072 * a + at
        return Z[:, base:base + n]

    SEL_ = [mb(a, 0, 256).rearrange("p (t s) -> p t s", t=NT) for a in range(3)]
    SELW = [mb(a, 256, 256).rearrange("p (t s) -> p t s", t=NT) for a in range(3)]
    XE = [mb(a, 512, 512).rearrange("p (c s) -> p c s", s=CAP) for a in range(3)]
    SWT = [mb(a, 1024, 256) for a in range(3)]
    SG = [mb(a, 1280, 512) for a in range(3)]
    HH = [mb(a, 1792, 512) for a in range(3)]
    HT = [mb(a, 2304, 256).rearrange("p (c s) -> p c s", s=CAP) for a in range(3)]
    YE = [mb(a, 2560, 512) for a in range(3)]
    RT = Z[:, 11264:12288]
    RANK = RT[:, 0:32].rearrange("p (t e) -> p t e", t=NT)
    COMB = RT[:, 32:64].rearrange("p (t e) -> p t e", t=NT)
    SELT = RT[:, 64:96].rearrange("p (t e) -> p t e", t=NT)
    RKX = RT[:, 96:98]
    B_XG, B_TR, B_GU, B_Y = 4, 5, 6, 7

    def m(L, name):
        return S(f"m{L}_{name}")

    def wait_expert(eng, L, name, v):
        v = v + L * (NE - 1 if name == "scat" else NE)
        if not isinstance(v, int) or v > 0:
            eng.wait_ge(S("expert_" + name), v)

    block = ctx.enter_context(nc.Block())
    NLAYER = sum(1 for k in order if k[0] == "moe")

    @block.tensor
    def _(pe):
        def mm(o, l, r, start, stop):
            return nc.tensor.matmul(o, l, r, start=start, stop=stop, skip_group_check=True)

        def transposes(key, src, chunks):
            for j in range((chunks + 1) // 2):
                o = claim(pe, (key, j), "B")
                for c in (2 * j, 2 * j + 1):
                    if c < chunks:
                        for t in range(NT):
                            at = (c % 2) * SEQ + t * P
                            ins = nc.tensor.transpose(o[:, at:at + P], src(t, c), ident)
                fill(ins, (key, j))

        def turned(key, chunks):
            for j in range((chunks + 1) // 2):
                read(pe, (key, j))

        def project(key, n=512):
            w = panel(pe, key, n)
            for t in range(NT):
                o = claim(pe, (key, t), "A")
                for c in range(KC):
                    ins = mm(o[:, 0:n], hT[:, c, t * P:(t + 1) * P], w[:, c, :], c == 0, c == KC - 1)
                fill(ins, (key, t))
            released(key, (key, NT - 1))

        def project_T(key):
            w = panel(pe, key, 512)
            for f in range(2):
                o = claim(pe, (key, f), "A")
                for g in range(2):
                    col = (2 * f + g) * P
                    for c in range(KC):
                        ins = mm(o[:, g * SEQ:(g + 1) * SEQ], w[:, c, col:col + P], hT[:, c, :], c == 0, c == KC - 1)
                fill(ins, (key, f))
            released(key, (key, 1))

        def out_project(key, panels, lhs, at=0):
            banks = {(t, h): claim(pe, (key, "o", t, h), "A") for t in range(NT) for h in range(2)}
            for j in range(panels):
                w = panel(pe, (key, j), D)
                for t in range(NT):
                    for h in range(2):
                        for c in range(4):
                            ins = mm(banks[t, h], lhs(4 * j + c)[:, t * P:(t + 1) * P], w[:, c, h * 512:(h + 1) * 512],
                                     j == 0 and c == 0, j == panels - 1 and c == 3)
                        if j == panels - 1:
                            fill(ins, (key, "o", t, h))
                if j < panels - 1:
                    op_reads[0] += 1
                    ins.then_inc(S("out_panel_read"), 1)
                    freed_by[(key, j)] = (S("out_panel_read"), op_reads[0])
                else:
                    released((key, j), (key, "o", NT - 1, 1))

        def released(key, last):
            b, k = where[last]
            freed_by[key] = (filled[b], k)

        pending = []

        def ada_flush():
            if pending:
                n = pending.pop()
                read(pe, ("ada", n))
                o = claim(pe, ("adac", n), "A")
                for f in range(4):
                    ins = mm(o[:, f:f + 1], AROW[:, f * P:(f + 1) * P], cst(C_PICK, 1), True, True)
                fill(ins, ("adac", n))

        def ada_panel(n):
            ada_flush()
            w = panel(pe, ("ada", n), 512)
            if n == 0:
                pe.wait_ge(S("silu_c"), 1)
            o = claim(pe, ("ada", n), "A")
            for c in range(KC):
                g = 32 * (c % 4)
                ins = mm(o[g:g + 32, :], SILC[:, c, :], w[:, c, :], c < 4, c >= 4)
            fill(ins, ("ada", n))
            released(("ada", n), ("ada", n))
            pending.append(n)

        pe.wait_ge(S("cst_in"), 16)
        pe.wait_ge(S("vec_in"), 16 * 8)
        for i in range(2):
            o = claim(pe, ("vec", i), "B")
            r = (60, 96)[i]
            fill(nc.tensor.transpose(o[:, 0:r], VROW[0:r, i, :], CST[0:r, C_ID:C_ID + r]), ("vec", i))
        pe.wait_ge(S("ws_in"), 16)
        o = claim(pe, ("ws", 0), "B")
        for g in range(4):
            ins = nc.tensor.transpose(o[:, g * P:(g + 1) * P], Z[:, 4096 + g * P:4096 + (g + 1) * P], ident)
        fill(ins, ("ws", 0))

        mn = Z[:, 2048:4096].rearrange("p (t d) -> p t d", t=NT)
        pe.wait_ge(S("xn_ready"), 1)
        transposes("mem", lambda t, c: mn[:, t, c * P:(c + 1) * P], KC)
        turned("mem", KC)
        project_T(("ckv", 0))
        project(("ckv", 1))

        pe.wait_ge(S("xn_ready"), 2)
        transposes("x", lambda t, c: XN[:, t, c * P:(c + 1) * P], KC)
        turned("x", KC)
        for nme, _, w in IN:
            project(("in", nme), w)

        def attention(tag, heads, q_at, k_at, v_at, half, fillers):
            def scores(h):
                o = claim(pe, (tag, "s", h), "B")
                for t in range(NT):
                    ins = mm(o[:, t * SEQ:(t + 1) * SEQ], q_at(h)[:, t * P:(t + 1) * P], k_at(h), t == 0, t == NT - 1)
                fill(ins, (tag, "s", h))

            def turn_probs(h):
                pe.wait_ge(S(f"{tag}_probs"), h + 1)
                o = claim(pe, (tag, "p", h), "B")
                pr = prob_buf[tag][h % 2]
                for c in range(2):
                    for t in range(NT):
                        ins = nc.tensor.transpose(o[:, c * SEQ + t * P:c * SEQ + (t + 1) * P],
                                                  pr[:, t, c * P:(c + 1) * P], ident)
                fill(ins, (tag, "p", h))

            def values(h):
                read(pe, (tag, "p", h))
                o = claim(pe, (tag, "v", h), "A")
                pt = probT_buf[tag][h % 2]
                rows = slice(64 * (h % 2), 64 * (h % 2) + 64) if half else slice(0, P)
                for c in range(2):
                    ins = mm(o[rows, 0:SEQ], v_at(h, c), pt[:, c * SEQ:(c + 1) * SEQ], c == 0, c == 1)
                fill(ins, (tag, "v", h))

            scores(0)
            for h in range(heads):
                if h + 1 < heads:
                    scores(h + 1)
                if h < len(fillers):
                    ada_panel(fillers[h])
                turn_probs(h)
                if h >= 1:
                    values(h - 1)
            values(heads - 1)
            ada_flush()

        pe.wait_ge(S("qk_roped"), 1)
        transposes("gq", lambda t, c: QR[:, t, c * P:(c + 1) * P], 4)
        transposes("gk", lambda t, c: KD[:, t, c * P:(c + 1) * P], 2)
        turned("gq", 4)
        turned("gk", 2)
        for t in range(NT):
            read(pe, (("in", "kv"), t))
        def half_rows(h):
            return slice(64 * (h % 2), 64 * (h % 2) + 64)
        attention("g", 8, lambda h: GQT[half_rows(h), h // 2, :], lambda h: GKT[half_rows(h), h // 4, :],
                  lambda h, c: GV[:, c, 64 * (h // 4):64 * (h // 4) + 64], True, list(range(8)))

        read(pe, ("ws", 0))
        for t in range(NT):
            pe.wait_ge(S("sv_normed"), t + 1)
            o = claim(pe, ("sgu", t), "A")
            for g in range(4):
                ins = mm(o[:, g * P:(g + 1) * P], WST[:, g, :], SV[:, t, g * P:(g + 1) * P], True, True)
            fill(ins, ("sgu", t))
        for t in range(NT):
            read(pe, ("sgu", t))
        transposes("sg", lambda t, c: SU[:, t, c * P:(c + 1) * P], 4)
        for h in range(8):
            read(pe, ("g", "v", h))
        out_project("att_out", 1, lambda c: hT[:, c, :])
        turned("sg", 4)
        out_project("sgu_out", 1, lambda c: hT[:, 4 + c, :])
        pe.wait_ge(S("merged"), 4)
        transposes("mg", lambda t, c: GA[:, t, c * P:(c + 1) * P], KC)
        turned("mg", KC)
        out_project("w_out", 2, lambda c: hT[:, c, :])

        pe.wait_ge(S("xn_ready"), 3)
        transposes("xc", lambda t, c: XN[:, t, c * P:(c + 1) * P], KC)
        turned("xc", KC)
        project_T(("cq", 0))
        for f in range(2):
            read(pe, (("cq", 0), f))
            read(pe, (("ckv", 0), f))
        for t in range(NT):
            read(pe, (("ckv", 1), t))
        attention("c", 4, lambda h: CQT[:, h, :], lambda h: MKT[:, h, :],
                  lambda h, c: MVV[:, c, h * P:(h + 1) * P], False, list(range(8, 12)))
        for h in range(4):
            read(pe, ("c", "v", h))
        out_project("co", 1, lambda c: hT[:, c, :])

        def moe(L):
            src = XN if L == 0 else X
            wr, nr = (WR1, 20) if L == 0 else (WR2, 16)
            if L == 0:
                pe.wait_ge(S("xn_ready"), 4)
            else:
                pe.wait_ge(S("x_ready"), 2 * L)
            transposes(("moe", L), lambda t, c: src[:, t, c * P:(c + 1) * P], KC)
            turned(("moe", L), KC)
            o = claim(pe, ("route", L), "B")
            for t in range(NT):
                for c in range(KC):
                    ins = mm(o[:, 32 * t:32 * t + nr], hT[:, c, t * P:(t + 1) * P], wr[:, c, :], c == 0, c == KC - 1)
            fill(ins, ("route", L))
            pe.wait_ge(m(L, "chosen"), 1)
            o = claim(pe, ("rank", L), "B")
            mm(o[:, 0:16], cst(C_PREFIX), SELT[:, 0, :], True, True)
            mm(o[:, 16:32], cst(C_PREFIX), SELT[:, 1, :], True, False)
            mm(o[:, 16:32], cst(C_ONES), SELT[:, 0, :], False, True)
            mm(o[:, 32:48], cst(C_ONES), SELT[:, 0, :], True, False)
            fill(mm(o[:, 32:48], cst(C_ONES), SELT[:, 1, :], False, True), ("rank", L))
            progress[0] += 1
            acc = [claim(pe, ("y", L, i), "A") for i in range(4)]
            for b in range(4, 8):
                pe.wait_ge(drained[b], uses[b])
            pe.wait_ge(m(L, "zero"), 1)
            for i in range(4):
                ins = mm(acc[i], YE[0][:, 0:P], YE[0], True, False)
            ins.then_inc(m(L, "xdone"), 1)
            base = first_of[("moe", L)]

            def gather(a, done):
                for c in range(KC):
                    for t in range(NT):
                        mm(ps[:, B_XG, c * CAP:(c + 1) * CAP], src[:, t, c * P:(c + 1) * P], SEL_[a][:, t, 0:CAP],
                           t == 0, t == NT - 1)
                for t in range(NT):
                    ins = nc.tensor.transpose(ps[:, B_TR, t * P:(t + 1) * P], SELW[a][:, t, :], ident)
                ins.then_inc(done, 1)

            def gate_up(a, wg, wu, done):
                for c in range(KC):
                    mm(ps[0:CAP, B_GU, :], XE[a][:, c, :], wg[:, c, :], c == 0, c == KC - 1)
                    ins = mm(ps[CAP:P, B_GU, :], XE[a][:, c, :], wu[:, c, :], c == 0, c == KC - 1)
                ins.then_inc(done, 1)

            def turn_h(a, done):
                for c in range(4):
                    ins = mm(ps[:, B_GU, c * CAP:(c + 1) * CAP],
                             HH[a][CAP:P, c * P:(c + 1) * P], CST[CAP:P, C_ID + CAP:C_ID + P], True, True)
                ins.then_inc(done, 1)

            def down(a, wd, done):
                for c in range(4):
                    mm(ps[0:CAP, B_Y, :], HT[a][:, c, :], wd[:, c, 0:512], c == 0, c == 3)
                    ins = mm(ps[CAP:P, B_Y, :], HT[a][:, c, :], wd[:, c, 512:1024], c == 0, c == 3)
                ins.then_inc(done, 1)

            def scatter(a, last):
                for t in range(NT):
                    for h in range(2):
                        r = slice(CAP * h, CAP * (h + 1))
                        ins = mm(acc[2 * t + h], SWT[a][r, t * P:(t + 1) * P], YE[a][r, :], False, last)
                        if last:
                            fill(ins, ("y", L, 2 * t + h))
                return ins

            def expert(e, i, a, first, final):
                s = [(base + PER * a + j) % RING for j in range(PER)]
                k = [(base + PER * a + j) // RING for j in range(PER)]
                wg = ring[:, s[0], :].rearrange("p (c n) -> p c n", n=512)
                wu = ring[:, s[1], :].rearrange("p (c n) -> p c n", n=512)
                wd = ring[:, s[2], :].rearrange("p (c n) -> p c n", n=D)
                wait_expert(pe, L, "xe", e + 1)
                wait_expert(pe, L, "h", e)
                for j in range(2):
                    pe.wait_ge(landed[s[j]], 16 * (i + k[j] + 1))
                gate_up(a, wg, wu, S("expert_gu"))
                if not first:
                    wait_expert(pe, L, "ye", e)
                    wait_expert(pe, L, "swt", e)
                    scatter(1 - a, False).then_inc(S("expert_scat"), 1)
                if not final:
                    wait_expert(pe, L, "sel", e + 2)
                    wait_expert(pe, L, "swt", e + 1)
                    gather(1 - a, S("expert_xg"))
                wait_expert(pe, L, "h", e + 1)
                wait_expert(pe, L, "ht", e)
                turn_h(a, S("expert_htp"))
                wait_expert(pe, L, "ht", e + 1)
                pe.wait_ge(landed[s[2]], 16 * (i + k[2] + 1))
                down(a, wd, S("expert_y"))
                nb = pe.value_load(TBL[0:1, L, 0, bass.ds(e, 1)], min_val=0, max_val=3)
                b1 = pe.value_load(TBL[0:1, L, 1, bass.ds(e, 1)], min_val=1, max_val=48)
                with pe.If(nb > 0):
                    with pe.Fori(0, nb) as j:
                        wait_expert(pe, L, "ye", e + 1)
                        if not final:
                            wait_expert(pe, L, "xe", e + 2)
                            wait_expert(pe, L, "swt", e + 2)
                        pe.wait_ge(m(L, "x_sel"), b1 + j)
                        gather(2, m(L, "x_xg"))
                        pe.wait_ge(m(L, "x_xe"), b1 + j)
                        gate_up(2, wg, wu, m(L, "x_gu"))
                        pe.wait_ge(m(L, "x_h"), b1 + j)
                        turn_h(2, m(L, "x_htp"))
                        pe.wait_ge(m(L, "x_ht"), b1 + j)
                        down(2, wd, m(L, "x_y"))
                        pe.wait_ge(m(L, "x_swt"), b1 + j)
                        pe.wait_ge(m(L, "x_ye"), b1 + j)
                        scatter(2, False).then_inc(m(L, "xdone"), 1)

            wait_expert(pe, L, "sel", 1)
            gather(0, S("expert_xg"))
            pe.wait_ge(m(L, "table"), 1)
            expert(0, 0, 0, True, False)
            expert(1, 0, 1, False, False)
            with pe.Fori(1, NE // 2 - 1) as i:
                for a in range(2):
                    expert(2 * i + a, i, a, False, False)
            expert(NE - 2, NE // 2 - 1, 0, False, False)
            expert(NE - 1, NE // 2 - 1, 1, False, True)
            wait_expert(pe, L, "ye", NE)
            wait_expert(pe, L, "swt", NE)
            scatter(1, True)

        if NLAYER > 0:
            moe(0)

        def gate_rows(s):
            pe.wait_ge(S("diag"), s + 1)
            for h in range(2):
                o = claim(pe, ("gate", s, h), "B")
                fill(mm(o, cst(C_ONES), GB[:, h * 512:(h + 1) * 512], True, True), ("gate", s, h))

        if ("sb", 0) in order:
            pe.wait_ge(S("x_ready"), 1)
            transposes("sbx", lambda t, c: X[:, t, c * P:(c + 1) * P], KC)
            turned("sbx", KC)
            for j in range(4):
                project_T(("sb", j))
            for j in range(4, 6):
                project(("sb", j))
            for j in range(4):
                for f in range(2):
                    read(pe, (("sb", j), f))
            gate_rows(0)

            def logits(key, h, pool, stop):
                o = claim(pe, key, pool)
                r = half_rows(h)
                mm(o[:, 0:256], SKT[r, h // 2, 0:P], SQT[r, h // 2, :], True, stop)
                fill(mm(o[:, 256:384], SKT[r, h // 2, P:SEQ], SQT[r, h // 2, P:SEQ], False, stop), key)

            for h in range(16):
                logits(("z1", h), h, "B", True)
                if h % 4 == 3 and h < 15:
                    ada_panel(12 + h // 4)
            for j in range(4, 6):
                for t in range(NT):
                    read(pe, (("sb", j), t))

            def accumulate(h):
                pe.wait_ge(S("sp"), h + 1)
                o = ps[:, where[("z2", h)][0], :]
                e = SE[:, h, :]
                mm(o[:, 0:256], cst(C_NEGU), e[:, 0:256], False, False)
                mm(o[:, 256:384], cst(C_NEGU), e[:, 256:384], False, False)
                mm(o[:, 128:256], cst(C_NEG1), e[:, 256:384], False, False)
                mm(o[:, 0:128], ident, cst(C_NEGMASK), False, False)
                mm(o[:, 256:384], ident, cst(C_NEGMASK), False, True).then_inc(S("logit"), 1)

            def sb_values(h):
                read(pe, ("z2", h))
                o = claim(pe, ("sv", h), "A")
                r = half_rows(h)
                mm(o[r, 0:256], SBV[:, 0, 64 * h:64 * h + 64], SE[:, h, 0:256], True, False)
                fill(mm(o[r, 128:256], SBV[:, 1, 64 * h:64 * h + 64], SE[:, h, 256:384], False, True), ("sv", h))

            logits(("z2", 0), 0, "B", False)
            logits(("z2", 1), 1, "B", False)
            for h in range(16):
                if h + 2 < 16:
                    logits(("z2", h + 2), h + 2, "B", False)
                accumulate(h)
                if h >= 1:
                    sb_values(h - 1)
                if h % 5 == 4:
                    ada_panel(15 + h // 5)
            sb_values(15)
            ada_flush()
            for h in range(16):
                read(pe, ("sv", h))
            out_project("sb_out", 2, lambda c: hT[:, c, :])
        if NLAYER > 1:
            gate_rows(1)
            moe(1)

        if ("ret", 0) in order:
            pe.wait_ge(S("x_ready"), 3)
            transposes("rx", lambda t, c: X[:, t, c * P:(c + 1) * P], KC)
            turned("rx", KC)
            for j in range(6):
                project(("ret", j))
            pe.wait_ge(S("ret_roped"), 1)
            transposes("rq", lambda t, c: RQ[:, t, c * P:(c + 1) * P], KC)
            transposes("rk", lambda t, c: RK[:, t, c * P:(c + 1) * P], KC)
            for j in range(6, 12):
                project(("ret", j))
            turned("rq", KC)
            turned("rk", KC)
            gate_rows(2)
            for j in range(4, 8):
                for t in range(NT):
                    read(pe, (("ret", j), t))

            def ret_scores(h):
                o = claim(pe, ("rs", h), "B")
                mm(o[:, 0:256], RKT[:, h, 0:P], RQT[:, h, :], True, False)
                fill(mm(o[:, 256:384], RKT[:, h, P:SEQ], RQT[:, h, P:SEQ], False, True), ("rs", h))

            def ret_values(h):
                read(pe, ("rs", h))
                o = claim(pe, ("rv", h), "A")
                s = SM[:, h % 2, :]
                mm(o[:, 0:256], s[:, 0:128], RV[:, 0, 256 * h:256 * h + 256], True, True)
                mm(o[:, 256:512], s[:, 128:256], RV[:, 0, 256 * h:256 * h + 256], True, False)
                fill(mm(o[:, 256:512], s[:, 256:384], RV[:, 1, 256 * h:256 * h + 256], False, True), ("rv", h))

            ret_scores(0)
            for h in range(8):
                if h < 7:
                    ret_scores(h + 1)
                if h < 6:
                    ada_panel(18 + h)
                ret_values(h)
            ada_flush()
            for h in range(8):
                read(pe, ("rv", h))
            pe.wait_ge(S("ret_gated"), 1)
            transposes("ro", lambda t, c: RG[:, t, c * P:(c + 1) * P], 16)
            turned("ro", 16)
            out_project("ret_out", 4, lambda c: ROT[:, c, :])
        if NLAYER > 2:
            gate_rows(3)
            moe(2)
        if stop is None:
            assert progress[0] == len(order)

    @block.sync
    def _(sp):
        def wait_moe_slot(L, e):
            sp.wait_ge(m(L, "table"), 1)
            wait_expert(sp, L, "y", e + 1)
            done = sp.value_load(TBL[0:1, L, 2, bass.ds(e, 1)], min_val=1, max_val=48)
            sp.wait_ge(m(L, "xdone"), done)

        def load(n, src, size):
            w = src.shape[2]
            sp.dma_start(ring[:, n % RING, 0:size].rearrange("p (c n) -> p c n", n=w), src).then_inc(landed[n % RING], 16)

        def wait_slot(n):
            if n < RING:
                return
            key, j = owner[n - RING]
            if key[0] == "moe":
                wait_moe_slot(key[1], j // PER)
            else:
                sp.wait_ge(*freed_by[key])

        for key, src in stream:
            n = first_of[key]
            if src:
                wait_slot(n)
                load(n, *src)
                continue
            L = key[1]
            wg, wu, wd = MOE_W[L]

            def expert_loads(e, a):
                for j, (w, pat) in enumerate(((wg, P), (wu, P), (wd, P))):
                    v = w[bass.ds(e, 1)].rearrange("o (c p) n -> p (o c) n", p=P)
                    load(n + PER * a + j, v, PAN)

            for a in range(2):
                for j in range(PER):
                    wait_slot(n + PER * a + j)
                    w = MOE_W[L][j]
                    load(n + PER * a + j, w[a:a + 1].rearrange("o (c p) n -> p (o c) n", p=P), PAN)
            with sp.Fori(1, NE // 2) as i:
                for a in range(2):
                    wait_moe_slot(L, 2 * i + (a - 2))
                    expert_loads(2 * i + a, a)
        sp.wait_ge(S("x_ready"), final_ready)
        sp.dma_start(out.rearrange("o (t p) d -> p (o t) d", p=P), X[:, :, :]).then_inc(S("stored"), 16)
        sp.wait_ge(S("stored"), 16)

    def bc(ap, shape, *axes):
        for a in axes:
            ap = ap.unsqueeze(a)
        return ap.broadcast_to([P] + list(shape))

    TURN = {
        "mem": (lambda c: VT[:, 0, V_MEM + c:V_MEM + c + 1], None), "x": (lambda c: VT[:, 0, V_MIX + c:V_MIX + c + 1], None),
        "xc": (lambda c: VT[:, 0, V_CROSS + c:V_CROSS + c + 1], None),
        ("moe", 0): (lambda c: VT[:, 0, V_MOE + c:V_MOE + c + 1], None),
        "ro": (lambda c: VT[:, 0, V_GN + c:V_GN + c + 1], None),
    }
    for tag, s in (("sbx", 0), (("moe", 1), 1), ("rx", 2), (("moe", 2), 3)):
        TURN[tag] = ((lambda s: lambda c: ADA[:, 24 * s + 8 + c:24 * s + 9 + c])(s), (lambda s: lambda c: ADA[:, 24 * s + c:24 * s + c + 1])(s))

    @block.scalar
    def _(act):
        Copy = ACT.Copy
        nc.scalar.dma_start(CST[:, :], A["cst"]).then_inc(S("cst_in"), 16)
        nc.scalar.dma_start(MEM, A["mem"][0].rearrange("(t p) d -> p t d", p=P)).then_inc(S("mem_in"), 16)
        rows = [(A["g_mix"], V_MIX, 8), (A["g_cross"], V_CROSS, 8), (A["g_mem"], V_MEM, 8), (A["g_moe"], V_MOE, 8),
                (A["c_2"], V_C, 8), (A["ret_gn_g_2"], V_GN, 16)]
        for v, r, k in rows:
            nc.scalar.dma_start(VROW[r:r + k, 0, :], v.rearrange("o (k p) -> (o k) p", p=P)).then_inc(S("vec_in"), 16)
        nc.scalar.dma_start(VROW[V_BS:V_BS + 4, 0, :], A["b_s"][0]).then_inc(S("vec_in"), 16)
        nc.scalar.dma_start(VROW[0:96, 1, :], A["ada_b_2"].rearrange("a b (k p) -> (a b k) p", p=P)).then_inc(S("vec_in"), 16)
        nc.scalar.dma_start(WSR.rearrange("p (g q) -> p g q", g=4), A["w_s"][0].rearrange("g p q -> p g q")).then_inc(S("ws_in"), 16)
        nc.scalar.dma_start(X[:, :, :], A["x"][0].rearrange("(t p) d -> p t d", p=P)).then_inc(S("x_in"), 16)
        nc.scalar.dma_start(POS[:, :], A["positions_2"][0].rearrange("(t p) -> p t", p=P), allow_slow_non_contiguous=True).then_inc(S("pos_in"), 16)
        small = [(GQK[:, 0:8, :], A["g_q"].unsqueeze(0).broadcast_to([P, 8, 64])), (GQK[:, 8:10, :], A["g_k"].unsqueeze(0).broadcast_to([P, 2, 64])),
                 (SGB[:, 0, :], A["sgu_ln_g"][0].partition_broadcast(P)), (SGB[:, 1, :], A["sgu_ln_b"][0].partition_broadcast(P)),
                 (WR1[:, :, 0:4], A["w_rg"][0].rearrange("(c p) n -> p c n", p=P)), (WR1[:, :, 4:20], A["w_re"][0].rearrange("(c p) n -> p c n", p=P)),
                 (WR2[:, :, :], A["router_w_2"].rearrange("(c p) n -> p c n", p=P)),
                 (BR1[:, 0:4], A["b_rg"][0].partition_broadcast(P)), (BR1[:, 4:20], A["b_re"][0].partition_broadcast(P)),
                 (BR2[:, :], A["router_b_2"].partition_broadcast(P))]
        for dst, src in small:
            nc.scalar.dma_start(dst, src).then_inc(S("small_in"), 16)

        def turn_out(key, chunks, dest):
            scale, shift = TURN.get(key, (None, None))
            for j in range(0, (chunks + 1) // 2, 2):
                o = result(act, (key, j))
                for c in (2 * j, 2 * j + 1):
                    i = o[:, (c % 2) * SEQ:(c % 2) * SEQ + SEQ]
                    if shift:
                        ins = nc.scalar.activation(dest(c), i, ACT.Identity, scale=scale(c), bias=shift(c))
                    elif scale:
                        ins = nc.scalar.activation(dest(c), i, Copy, scale=scale(c))
                    else:
                        ins = nc.scalar.activation(dest(c), i, Copy)
                drain(ins, (key, j))

        def move(key, dst, src=slice(0, 512), func=Copy, **k):
            o = result(act, key)
            drain(nc.scalar.activation(dst, o[:, src], func, **k), key)

        def halves(v):
            return v.rearrange("p a b -> p (a b)")

        read(act, ("vec", 0))
        nc.scalar.activation(SILC[:, :, :], bc(VT[:, 0, V_C:V_C + 8], [8, 32], 2), ACT.Silu).then_inc(S("silu_c"), 1)
        act.wait_ge(S("angles"), 1)
        nc.scalar.activation(CS2[:, :, :, :].rearrange("p a t i -> p a (t i)"), RR, ACT.Sin).then_inc(S("cos_sin"), 1)
        turn_out("mem", KC, lambda c: hT[:, c, :])
        for f in range(2):
            move((("ckv", 0), f), halves(MKT[:, 2 * f:2 * f + 2, :]))
        for t in range(NT):
            move((("ckv", 1), t), MVV[:, t, :])
        turn_out("x", KC, lambda c: hT[:, c, :])
        for t in range(NT):
            move((("in", "q"), t), QK5[:, t, 0:512])
        for t in range(NT):
            o = result(act, (("in", "kv"), t))
            nc.scalar.activation(GV[:, t, :], o[:, 128:256], Copy)
            drain(nc.scalar.activation(QK5[:, t, 512:640], o[:, 0:128], Copy), (("in", "kv"), t))
        for nme, v in (("su", SU), ("sv", SV)):
            for t in range(NT):
                move((("in", nme), t), v[:, t, :], func=ACT.Gelu_apprx_tanh)
        for nme, v, h in (("ga0", GA, 0), ("ga1", GA, 1), ("gb0", GBT, 0), ("gb1", GBT, 1)):
            for t in range(NT):
                move((("in", nme), t), v[:, t, 512 * h:512 * h + 512], func=ACT.Sigmoid)
        turn_out("gq", 4, lambda c: GQT[:, c, :])
        turn_out("gk", 2, lambda c: GKT[:, c, :])

        def ada_copy(n):
            move(("ada", n), AROW[:, :])

        def attention(tag, heads, scale, fillers):
            def exps(h):
                act.wait_ge(S(f"{tag}_max"), h + 1)
                if h >= 2:
                    result(act, (tag, "p", h - 2))
                o = result(act, (tag, "s", h))
                for t in range(NT):
                    ins = nc.scalar.activation(prob_buf[tag][h % 2][:, t, :], o[:, t * SEQ:(t + 1) * SEQ], ACT.Exp,
                                               bias=SX[:, h % 2, 0, t:t + 1], scale=scale, accum_out=SX[:, h % 2, 1, t:t + 1])
                drain(ins, (tag, "s", h))

            exps(0)
            for h in range(heads):
                if h + 1 < heads:
                    exps(h + 1)
                if h < len(fillers):
                    ada_copy(fillers[h])
                if h >= 2:
                    result(act, (tag, "v", h - 2))
                move((tag, "p", h), probT_buf[tag][h % 2])

        attention("g", 8, ATT_SCALE, list(range(8)))
        turn_out("sg", 4, lambda c: hT[:, 4 + c, :])
        turn_out("mg", KC, lambda c: hT[:, c, :])
        turn_out("xc", KC, lambda c: hT[:, c, :])
        for f in range(2):
            move((("cq", 0), f), halves(CQT[:, 2 * f:2 * f + 2, :]))
        attention("c", 4, X_SCALE, list(range(8, 12)))

        def moe(L):
            if L > 0:
                act.wait_ge(S("ada_set"), 2 * L)
            turn_out(("moe", L), KC, lambda c: hT[:, c, :])
            if L == 0:
                act.wait_ge(m(L, "rt0"), 1)
                nc.scalar.activation(RT[:, 128:136], RT[:, 128:136], ACT.Exp).then_inc(m(L, "re0"), 1)
            else:
                act.wait_ge(m(L, "rt0"), 1)
                nc.scalar.activation(RT[:, 128:160], RT[:, 128:160], ACT.Exp).then_inc(m(L, "re0"), 1)
            act.wait_ge(m(L, "rt1"), 1)
            nc.scalar.activation(RT[:, 224:226], RT[:, 224:226], ACT.Exp).then_inc(m(L, "re1"), 1)

            def swt_out(a, done):
                nc.scalar.activation(SWT[a], ps[:, B_TR, 0:SEQ], Copy).then_inc(done, 1)

            def silu(a, done):
                nc.scalar.activation(SG[a][CAP:P, :], ps[0:CAP, B_GU, :], ACT.Silu).then_inc(done, 1)

            def ht_out(a, done):
                nc.scalar.activation(HT[a].rearrange("p c s -> p (c s)"), ps[:, B_GU, 0:SEQ], Copy).then_inc(done, 1)

            def expert(e, a, final):
                wait_expert(act, L, "gu", e + 1)
                wait_expert(act, L, "h", e - 1)
                silu(a, S("expert_sg"))
                if not final:
                    wait_expert(act, L, "xg", e + 2)
                    wait_expert(act, L, "scat", e)
                    swt_out(1 - a, S("expert_swt"))
                wait_expert(act, L, "htp", e + 1)
                wait_expert(act, L, "y", e - 1)
                ht_out(a, S("expert_ht"))
                nb = act.value_load(TBL[0:1, L, 0, bass.ds(e, 1)], min_val=0, max_val=3)
                b1 = act.value_load(TBL[0:1, L, 1, bass.ds(e, 1)], min_val=1, max_val=48)
                with act.If(nb > 0):
                    with act.Fori(0, nb) as j:
                        act.wait_ge(m(L, "x_xg"), b1 + j)
                        act.wait_ge(m(L, "xdone"), b1 + j)
                        swt_out(2, m(L, "x_swt"))
                        act.wait_ge(m(L, "x_gu"), b1 + j)
                        silu(2, m(L, "x_sg"))
                        act.wait_ge(m(L, "x_htp"), b1 + j)
                        ht_out(2, m(L, "x_ht"))

            wait_expert(act, L, "xg", 1)
            swt_out(0, S("expert_swt"))
            act.wait_ge(m(L, "table"), 1)
            expert(0, 0, False)
            expert(1, 1, False)
            with act.Fori(1, NE // 2 - 1) as i:
                for a in range(2):
                    expert(2 * i + a, a, False)
            expert(NE - 2, 0, False)
            expert(NE - 1, 1, True)

        def gate_out(s):
            for h in range(2):
                move(("gate", s, h), GB[:, h * 512:(h + 1) * 512])

        if NLAYER > 0:
            moe(0)
        if ("sb", 0) in order:
            act.wait_ge(S("ada_set"), 1)
            turn_out("sbx", KC, lambda c: hT[:, c, :])
            for j in range(4):
                for f in range(2):
                    q = 4 * (j % 2) + 2 * f
                    move((("sb", j), f), halves((SQT if j < 2 else SKT)[:, q:q + 2, :]), scale=(ATT_SCALE if j < 2 else 1.0))
            for j in range(4, 6):
                for t in range(NT):
                    move((("sb", j), t), SBV[:, t, 512 * (j - 4):512 * (j - 3)])
            gate_out(0)
            for h in range(16):
                move(("z1", h), SE[:, h, :], slice(0, 384), ACT.Abs)
                if h % 4 == 3:
                    if h < 15:
                        ada_copy(12 + h // 4)
                    read(act, ("z1", h))
                    g = SE[:, h - 3:h + 1, :]
                    nc.scalar.activation(g, g, ACT.Exp, scale=-1.0).then_inc(S("exp_abs"), 1)
            for q in range(4):
                act.wait_ge(S("exp_abs"), q + 1)
                g = SE[:, 4 * q:4 * q + 4, :]
                nc.scalar.activation(g, g, ACT.Ln, bias=1.0).then_inc(S("log1p"), 1)
            for h in range(16):
                act.wait_ge(S("logit"), h + 1)
                move(("z2", h), SE[:, h, :], slice(0, 384), ACT.Exp)
                if h % 5 == 4:
                    ada_copy(15 + h // 5)
        if NLAYER > 1:
            gate_out(1)
            moe(1)
        if ("ret", 0) in order:
            act.wait_ge(S("ada_set"), 3)
            turn_out("rx", KC, lambda c: hT[:, c, :])
            for j in range(4):
                for t in range(NT):
                    move((("ret", j), t), (RQRAW if j < 2 else RKRAW)[:, t, 512 * (j % 2):512 * (j % 2) + 512])
            act.wait_ge(S("ret_roped"), 1)
            for j in range(4, 6):
                for t in range(NT):
                    move((("ret", j), t), RV[:, t, 512 * (j - 4):512 * (j - 3)])
            turn_out("rq", KC, lambda c: RQT[:, c, :])
            turn_out("rk", KC, lambda c: RKT[:, c, :])
            for j in range(6, 8):
                for t in range(NT):
                    move((("ret", j), t), RV[:, t, 512 * (j - 4):512 * (j - 3)])
            for j in range(8, 12):
                for t in range(NT):
                    move((("ret", j), t), RG[:, t, 512 * (j - 8):512 * (j - 7)], func=ACT.Silu)
            gate_out(2)
            for h in range(6):
                ada_copy(18 + h)
            turn_out("ro", 16, lambda c: ROT[:, c, :])
        if NLAYER > 2:
            gate_out(3)
            moe(2)

    norms = []
    @block.vector
    def _(dve):
        V = nc.vector
        chain = [0]

        def link(ins):
            chain[0] += 1
            ins.then_inc(S("dve"), 1)
            dve.wait_ge(S("dve"), chain[0])

        def power(n, par):
            norms.append((n, par))

        def rstd(k):
            dve.wait_ge(S("rstd"), k)

        def moments(x, width, eps, rms, par=0):
            k = max(1, width // 512)
            for t in range(NT):
                for i in range(k):
                    w = width // k
                    ins = V.bn_stats(ST[:, par, t, i, :], x(t)[:, i * w:(i + 1) * w])
            link(ins)
            for t in range(NT):
                ins = V.bn_aggr(MV[:, par, t, :], ST[:, par, t, 0:k, :])
            link(ins)
            mean, var = MV[:, par, :, 0], MV[:, par, :, 1]
            if rms:
                link(V.tensor_tensor(MS[:, par, 0:NT], mean, mean, ALU.mult))
                ins = V.scalar_tensor_tensor(out=MS[:, par, 0:NT], in0=MS[:, par, 0:NT], scalar=eps, in1=var, op0=ALU.add, op1=ALU.add)
            else:
                ins = V.tensor_scalar(MS[:, par, 0:NT], var, eps, None, ALU.add)
            ins.then_inc(S("square"), 1)
            power(NT, par)
            return len(norms)

        def rms_to(dst, x, done):
            rstd(moments(lambda t: x[:, t, :], D, EPS_RMS, True))
            for t in range(NT):
                ins = V.tensor_scalar(dst[:, t, :], x[:, t, :], RS[:, 0, t:t + 1], None, ALU.mult)
            ins.then_inc(done, 1)

        def turn_out(key, chunks, dest):
            scale, shift = TURN.get(key, (None, None))
            for j in range(1, (chunks + 1) // 2, 2):
                o = result(dve, (key, j))
                for c in (2 * j, 2 * j + 1):
                    i = o[:, (c % 2) * SEQ:(c % 2) * SEQ + SEQ]
                    if shift:
                        ins = V.tensor_scalar(dest(c), i, scale(c), shift(c), ALU.mult, ALU.add)
                    elif scale:
                        ins = V.tensor_scalar(dest(c), i, scale(c), None, ALU.mult)
                    else:
                        ins = V.tensor_copy(dest(c), i)
                drain(ins, (key, j))

        dve.wait_ge(S("mem_in"), 16)
        rms_to(MEMN, MEM, S("xn_ready"))
        for i, r in enumerate((60, 96)):
            o = result(dve, ("vec", i))
            drain(V.tensor_copy(VT[:, i, 0:r], o[:, 0:r]), ("vec", i))
        o = result(dve, ("ws", 0))
        drain(V.tensor_copy(WST[:, :, :].rearrange("p g q -> p (g q)"), o), ("ws", 0))
        dve.wait_ge(S("pos_in"), 16)
        dve.wait_ge(S("cst_in"), 16)
        link(V.tensor_copy(POSF[:, :], POS[:, :]))
        link(V.tensor_tensor(ANG.rearrange("p (t i) -> p t i", t=NT), bc(POSF[:, :], [NT, 64], 2), bc(cst(C_INVF, 64), [NT, 64], 1), ALU.mult))
        V.tensor_scalar(KK[:, 0, :], ANG, 1.0 / (2 * np.pi), 0.25, ALU.mult, ALU.add)
        link(V.tensor_scalar(KK[:, 1, :], ANG, 1.0 / (2 * np.pi), None, ALU.mult))
        magic = 1.5 * 2.0 ** 23
        link(V.tensor_scalar(KK, KK, magic, None, ALU.add))
        link(V.tensor_scalar(KK, KK, magic, None, ALU.subtract))
        link(V.scalar_tensor_tensor(out=RR, in0=KK, scalar=-6.28125, in1=bc(ANG, [2, 128], 1), op0=ALU.mult, op1=ALU.add))
        link(V.scalar_tensor_tensor(out=RR, in0=KK, scalar=-(2 * np.pi - 6.28125), in1=RR, op0=ALU.mult, op1=ALU.add))
        link(V.tensor_scalar(RR[:, 0, :], RR[:, 0, :], np.pi / 2, None, ALU.add))
        V.tensor_scalar(RR, RR, 3.1415925, -3.1415925, ALU.min, ALU.max).then_inc(S("angles"), 1)

        turn_out("mem", KC, lambda c: hT[:, c, :])
        dve.wait_ge(S("x_in"), 16)
        result(dve, ("mem", 3))
        rms_to(XN, X, S("xn_ready"))
        turn_out("x", KC, lambda c: hT[:, c, :])

        dve.wait_ge(S("small_in"), 16 * 10)
        for t in range(NT):
            read(dve, (("in", "q"), t))
            read(dve, (("in", "kv"), t))
        qk4 = QK5.rearrange("p t (h d) -> p t h d", d=64)
        link(V.tensor_tensor(R5, QK5, QK5, ALU.mult))
        link(V.tensor_reduce(MS[:, 1, 0:20].rearrange("p (t h) -> p t h", t=NT), R5.rearrange("p t (h d) -> p t h d", d=64), AX, ALU.add))
        V.tensor_scalar(MS[:, 1, 0:20], MS[:, 1, 0:20], 1.0 / 64, EPS_RMS, ALU.mult, ALU.add).then_inc(S("square"), 1)
        power(20, 1)
        rstd(len(norms))
        for t in range(NT):
            ins = V.tensor_tensor(qk4[:, t], qk4[:, t], bc(RS[:, 1, 10 * t:10 * t + 10], [10, 64], 2), ALU.mult)
        link(ins)
        link(V.tensor_tensor(QK5, QK5, bc(GQK[:, :, :].rearrange("p h d -> p (h d)"), [NT, 640], 1), ALU.mult))
        pairs = QK5.rearrange("p t (h i two) -> p t h i two", two=2, i=32)
        rot = R5.rearrange("p t (h i two) -> p t h i two", two=2, i=32)
        for t in range(NT):
            cos = bc(cst(C_ROPE + 64 * t, 32), [10, 32], 1)
            sin = bc(cst(C_ROPE + 64 * t + 32, 32), [10, 32], 1)
            x0, x1 = pairs[:, t, :, :, 0], pairs[:, t, :, :, 1]
            t1 = TMP[:, 0, 0:320].rearrange("p (h i) -> p h i", i=32)
            t2 = TMP[:, 1, 0:320].rearrange("p (h i) -> p h i", i=32)
            for o, c1, c2, op in ((rot[:, t, :, :, 0], cos, sin, ALU.subtract), (rot[:, t, :, :, 1], sin, cos, ALU.add)):
                V.tensor_tensor(t1, x0, c1, ALU.mult)
                link(V.tensor_tensor(t2, x1, c2, ALU.mult))
                link(V.tensor_tensor(o, t1, t2, op))
        for t in range(NT):
            for r in range(2):
                kd = KD[:, t, :].rearrange("p (v r d) -> p v r d", v=2, r=2)
                ins = V.tensor_copy(kd[:, :, r, :], R5[:, t, 512:640].rearrange("p (v d) -> p v d", v=2))
        ins.then_inc(S("qk_roped"), 1)
        for t in range(NT):
            read(dve, (("in", "sv"), t))
        rstd(moments(lambda t: SV[:, t, :], 512, EPS_RMS, False))
        for t in range(NT):
            link(V.tensor_scalar(SV[:, t, :], SV[:, t, :], MV[:, 0, t, 0:1], RS[:, 0, t:t + 1], ALU.subtract, ALU.mult))
            link(V.tensor_tensor(SV[:, t, :], SV[:, t, :], SGB[:, 0, :], ALU.mult))
            V.tensor_tensor(SV[:, t, :], SV[:, t, :], SGB[:, 1, :], ALU.add).then_inc(S("sv_normed"), 1)
        turn_out("gq", 4, lambda c: GQT[:, c, :])

        def ada_sum(n):
            o = result(dve, ("adac", n))
            drain(V.tensor_tensor(ADA[:, 4 * n:4 * n + 4], o[:, 0:4], VT[:, 1, 4 * n:4 * n + 4], ALU.add), ("adac", n))
            if n % 6 == 5:
                read(dve, ("adac", n))
                v = ADA[:, 4 * n - 12:4 * n + 4]
                V.tensor_scalar(v, v, 1.0, None, ALU.add).then_inc(S("ada_set"), 1)

        def attention(tag, heads, scale, fillers, out_rows):
            def maxima(h):
                o = result(dve, (tag, "s", h))
                link(V.tensor_reduce(SX[:, h % 2, 0, :], o.rearrange("p (t k) -> p t k", t=NT), AX, ALU.max))
                V.tensor_scalar(SX[:, h % 2, 0, :], SX[:, h % 2, 0, :], -scale, None, ALU.mult).then_inc(S(f"{tag}_max"), 1)

            def normalise(h):
                read(dve, (tag, "s", h))
                link(V.reciprocal(SX[:, h % 2, 2, :], SX[:, h % 2, 1, :]))
                for t in range(NT):
                    pr = prob_buf[tag][h % 2][:, t, :]
                    ins = V.tensor_scalar(pr, pr, SX[:, h % 2, 2, t:t + 1], None, ALU.mult)
                ins.then_inc(S(f"{tag}_probs"), 1)

            def values_out(h):
                o = result(dve, (tag, "v", h))
                dst, rows = out_rows(h)
                drain(V.tensor_copy(dst, o[rows, 0:SEQ]), (tag, "v", h))

            maxima(0)
            for h in range(heads):
                if h + 1 < heads:
                    maxima(h + 1)
                normalise(h)
                if 1 <= h <= len(fillers):
                    ada_sum(fillers[h - 1])
                if h >= 1:
                    values_out(h - 1)
            values_out(heads - 1)
            if len(fillers) >= heads:
                ada_sum(fillers[heads - 1])

        def half_rows(h):
            return slice(64 * (h % 2), 64 * (h % 2) + 64)
        attention("g", 8, ATT_SCALE, list(range(8)), lambda h: (hT[half_rows(h), h // 2, :], half_rows(h)))
        for t in range(NT):
            read(dve, (("in", "su"), t))
            o = result(dve, ("sgu", t))
            for g in range(4):
                v = SU[:, t, g * P:(g + 1) * P]
                ins = V.scalar_tensor_tensor(out=v, in0=o[:, g * P:(g + 1) * P], scalar=VT[:, 0, V_BS + g:V_BS + g + 1], in1=v, op0=ALU.add, op1=ALU.mult)
            drain(ins, ("sgu", t))
        turn_out("sg", 4, lambda c: hT[:, 4 + c, :])
        for t in range(NT):
            for h in range(2):
                read(dve, (("in", f"ga{h}"), t))
                v = GA[:, t, 512 * h:512 * h + 512]
                drain(V.tensor_tensor(v, result(dve, ("att_out", "o", t, h)), v, ALU.mult), ("att_out", "o", t, h))
        for t in range(NT):
            for h in range(2):
                read(dve, (("in", f"gb{h}"), t))
                v, g = GBT[:, t, 512 * h:512 * h + 512], GA[:, t, 512 * h:512 * h + 512]
                drain(V.tensor_tensor(v, result(dve, ("sgu_out", "o", t, h)), v, ALU.mult), ("sgu_out", "o", t, h))
                read(dve, ("sgu_out", "o", t, h))
                read(dve, ("att_out", "o", t, h))
                V.tensor_tensor(g, g, v, ALU.add).then_inc(S("merged"), 1)
        turn_out("mg", KC, lambda c: hT[:, c, :])

        def residual(keys):
            for t in range(NT):
                for h in range(2):
                    v = X[:, t, 512 * h:512 * h + 512]
                    drain(V.tensor_tensor(v, result(dve, keys(t, h)), v, ALU.add), keys(t, h))
            for t in range(NT):
                for h in range(2):
                    read(dve, keys(t, h))

        residual(lambda t, h: ("w_out", "o", t, h))
        rms_to(XN, X, S("xn_ready"))
        turn_out("xc", KC, lambda c: hT[:, c, :])
        attention("c", 4, X_SCALE, list(range(8, 12)), lambda h: (hT[:, h, :], slice(0, P)))
        residual(lambda t, h: ("co", "o", t, h))

        def top_two(L, logits, gidx):
            oh = RT[:, 160:192].rearrange("p (t e) -> p t e", t=NT)
            em = RT[:, 192:224].rearrange("p (t e) -> p t e", t=NT)
            link(V.tensor_tensor(oh, bc(cst(C_GRP, 16), [NT, 16], 1), gidx.broadcast_to([P, NT, 16]), ALU.is_equal))
            link(V.tensor_tensor(em, logits, oh, ALU.mult))
            link(V.tensor_scalar(oh, oh, BIG, -BIG, ALU.mult, ALU.add))
            link(V.tensor_tensor(em, em, oh, ALU.add))
            v8 = RT[:, 232:248].rearrange("p (t e) -> p t e", t=NT)
            for t in range(NT):
                link(V.max(v8[:, t, :], em[:, t, :]))
                link(V.max_index(RTI[:, 1, t, :], v8[:, t, :], em[:, t, :]))
            V.tensor_tensor(RT[:, 224:226], v8[:, :, 1], v8[:, :, 0], ALU.subtract).then_inc(m(L, "rt1"), 1)

        def moe(L):
            if L == 0:
                rms_to(XN, X, S("xn_ready"))
            turn_out(("moe", L), KC, lambda c: hT[:, c, :])
            nr = 20 if L == 0 else 16
            o = result(dve, ("route", L))[:, 0:64].rearrange("p (t e) -> p t e", t=NT)[:, :, 0:nr]
            lg = RT[:, 256:256 + 2 * nr].rearrange("p (t e) -> p t e", t=NT)
            drain(V.tensor_tensor(lg, o, bc((BR1 if L == 0 else BR2)[:, :], [NT, nr], 1), ALU.add), ("route", L))
            read(dve, ("route", L))
            pad = RT[:, 304:320].rearrange("p (t e) -> p t e", t=NT)
            g8 = RT[:, 320:336].rearrange("p (t e) -> p t e", t=NT)
            gsum, gval = RT[:, 336:338], RT[:, 338:340]
            link(V.memset(pad, -BIG))
            if L == 0:
                el = lg[:, :, 4:20]
                link(V.tensor_copy(pad[:, :, 0:4], lg[:, :, 0:4]))
            else:
                el = lg
                l8 = RT[:, 340:356].rearrange("p (t e) -> p t e", t=NT)
                for t in range(NT):
                    link(V.max(l8[:, t, :], lg[:, t, :]))
                pr = RT[:, 128:160].rearrange("p (t e) -> p t e", t=NT)
                V.tensor_tensor(pr, lg, l8[:, :, 0:1].broadcast_to([P, NT, 16]), ALU.subtract).then_inc(m(L, "rt0"), 1)
                dve.wait_ge(m(L, "re0"), 1)
                link(V.tensor_reduce(gsum, pr, AX, ALU.add))
                link(V.reciprocal(gval, gsum))
                link(V.tensor_tensor(pr, pr, gval.unsqueeze(2).broadcast_to([P, NT, 16]), ALU.mult))
                q = RT[:, 128:160].rearrange("p (g k) -> p g k", k=4)
                pairs_ = RT[:, 360:408].rearrange("p (g k) -> p g k", k=6)
                V.tensor_tensor(pairs_[:, :, 0:3], q[:, :, 0:3], q[:, :, 1:4], ALU.add)
                V.tensor_tensor(pairs_[:, :, 3:5], q[:, :, 0:2], q[:, :, 2:4], ALU.add)
                link(V.tensor_tensor(pairs_[:, :, 5:6], q[:, :, 0:1], q[:, :, 3:4], ALU.add))
                gs = RT[:, 408:416]
                link(V.tensor_reduce(gs, pairs_, AX, ALU.max))
                link(V.tensor_copy(pad[:, :, 0:4], gs.rearrange("p (t g) -> p t g", t=NT)))
            for t in range(NT):
                link(V.max(g8[:, t, :], pad[:, t, :]))
                link(V.max_index(RTI[:, 0, t, :], g8[:, t, :], pad[:, t, :]))
            gidx = RT[:, 356:358]
            link(V.tensor_copy(gidx, RTI[:, 0, :, 0]))
            if L == 0:
                ex = RT[:, 128:136].rearrange("p (t e) -> p t e", t=NT)
                V.tensor_tensor(ex, lg[:, :, 0:4], g8[:, :, 0:1].broadcast_to([P, NT, 4]), ALU.subtract).then_inc(m(L, "rt0"), 1)
                dve.wait_ge(m(L, "re0"), 1)
                link(V.tensor_reduce(gsum, ex, AX, ALU.add))
                link(V.reciprocal(gval, gsum))
            top_two(L, el, gidx.unsqueeze(2))
            i2 = RT[:, 420:424].rearrange("p (t k) -> p t k", t=NT)
            link(V.tensor_copy(i2, RTI[:, 1, :, 0:2]))
            o1 = RT[:, 424:456].rearrange("p (t e) -> p t e", t=NT)
            o2 = RT[:, 456:488].rearrange("p (t e) -> p t e", t=NT)
            V.tensor_tensor(o1, bc(cst(C_EXP, 16), [NT, 16], 1), i2[:, :, 0:1].broadcast_to([P, NT, 16]), ALU.is_equal)
            link(V.tensor_tensor(o2, bc(cst(C_EXP, 16), [NT, 16], 1), i2[:, :, 1:2].broadcast_to([P, NT, 16]), ALU.is_equal))
            V.tensor_tensor(SELT, o1, o2, ALU.add).then_inc(m(L, "chosen"), 1)
            dve.wait_ge(m(L, "re1"), 1)
            w1, w2 = RT[:, 226:228], RT[:, 228:230]
            link(V.tensor_scalar(w1, RT[:, 224:226], 1.0, None, ALU.add))
            link(V.reciprocal(w1, w1))
            if L == 0:
                link(V.tensor_tensor(w1, w1, gval, ALU.mult))
            link(V.tensor_tensor(w2, w1, RT[:, 224:226], ALU.mult))
            V.tensor_tensor(o1, o1, w1.unsqueeze(2).broadcast_to([P, NT, 16]), ALU.mult)
            link(V.tensor_tensor(o2, o2, w2.unsqueeze(2).broadcast_to([P, NT, 16]), ALU.mult))
            link(V.tensor_tensor(COMB, o1, o2, ALU.add))
            V.memset(YE[0], 0.0).then_inc(m(L, "zero"), 1)
            dve.wait_ge(m(L, "chosen"), 1)
            o = result(dve, ("rank", L))
            V.tensor_copy(TBF[0:1, 0, :], o[0:1, 32:48])
            link(V.scalar_tensor_tensor(out=RANK, in0=o[:, 0:32].rearrange("p (t e) -> p t e", t=NT), scalar=1.0, in1=SELT, op0=ALU.add, op1=ALU.mult))
            drain(V.tensor_scalar(RANK, RANK, -1.0, None, ALU.add), ("rank", L))
            read(dve, ("rank", L))
            for b in range(1, 4):
                ins = V.tensor_scalar(TBF[0:1, b, :], TBF[0:1, 0, :], b * CAP + 0.5, None, ALU.is_gt)
            link(ins)
            link(V.tensor_tensor(TBF[0:1, 4, :], TBF[0:1, 1, :], TBF[0:1, 2, :], ALU.add))
            link(V.tensor_tensor(TBF[0:1, 4, :], TBF[0:1, 4, :], TBF[0:1, 3, :], ALU.add))
            link(V.memset(TBF[0:1, 6, :], 1.0))
            link(V.tensor_tensor_scan(TBF[0:1, 5, :], TBF[0:1, 6, :], TBF[0:1, 4, :], 1.0, ALU.mult, ALU.add))
            link(V.tensor_tensor(TBF[0:1, 7, :], TBF[0:1, 5, :], TBF[0:1, 4, :], ALU.subtract))
            V.tensor_copy(TBL[0:1, L, 0, :], TBF[0:1, 4, :])
            V.tensor_copy(TBL[0:1, L, 1, :], TBF[0:1, 7, :])
            V.tensor_copy(TBL[0:1, L, 2, :], TBF[0:1, 5, :]).then_inc(m(L, "table"), 1)
            slots = cst(C_SLOT)
            if L == 0:
                gain, shift = VT[:, 0, V_MOE:V_MOE + 8], None
            else:
                s = 24 * (2 * L - 1)
                gain, shift = ADA[:, s + 8:s + 16], ADA[:, s:s + 8]

            def choose(a, rank, e, done):
                for t in range(NT):
                    V.tensor_scalar(SEL_[a][:, t, 0:CAP], slots[:, 0:CAP], rank(t), None, ALU.is_equal)
                    ins = V.tensor_scalar(SELW[a][:, t, :], slots, rank(t), COMB[:, t, bass.ds(e, 1)], ALU.is_equal, ALU.mult)
                ins.then_inc(done, 1)

            def ranks(e):
                return lambda t: RANK[:, t, bass.ds(e, 1)]

            def xe_out(a, done, mid, at):
                xg = ps[:, B_XG, :].rearrange("p (c s) -> p c s", s=CAP)
                gs_ = gain.unsqueeze(2).broadcast_to([P, KC, CAP])
                if shift is None:
                    V.tensor_tensor(XE[a], xg, gs_, ALU.mult).then_inc(done, 1)
                    return
                V.tensor_tensor(XE[a], xg, gs_, ALU.mult).then_inc(mid, 1)
                dve.wait_ge(mid, at)
                V.tensor_tensor(XE[a], XE[a], shift.unsqueeze(2).broadcast_to([P, KC, CAP]), ALU.add).then_inc(done, 1)

            def hidden(a, done):
                V.tensor_tensor(HH[a][CAP:P, :], ps[CAP:P, B_GU, :], SG[a][CAP:P, :], ALU.mult).then_inc(done, 1)

            def ye_out(a, done):
                V.tensor_copy(YE[a], ps[:, B_Y, :]).then_inc(done, 1)

            def expert(e, a, build_next, final):
                wait_expert(dve, L, "sg", e + 1)
                wait_expert(dve, L, "htp", e - 1)
                hidden(a, S("expert_h"))
                if build_next:
                    wait_expert(dve, L, "xg", e + 1)
                    choose(a, ranks(e + 2), e + 2, S("expert_sel"))
                if not final:
                    wait_expert(dve, L, "xg", e + 2)
                    wait_expert(dve, L, "gu", e)
                    xe_out(1 - a, S("expert_xe"), S("expert_xm"), NE * (L - 1) + e + 2)
                wait_expert(dve, L, "y", e + 1)
                wait_expert(dve, L, "scat", e - 1)
                ye_out(a, S("expert_ye"))
                nb = dve.value_load(TBL[0:1, L, 0, bass.ds(e, 1)], min_val=0, max_val=3)
                b1 = dve.value_load(TBL[0:1, L, 1, bass.ds(e, 1)], min_val=1, max_val=48)
                with dve.If(nb > 0):
                    with dve.Fori(0, nb) as j:
                        V.tensor_tensor(RKX.unsqueeze(2), RANK[:, :, bass.ds(e, 1)], CST[:, bass.ds(C_OFF + j, 1)].unsqueeze(1).broadcast_to([P, NT, 1]), ALU.subtract).then_inc(m(L, "x_rk"), 1)
                        dve.wait_ge(m(L, "x_rk"), b1 + j)
                        choose(2, lambda t: RKX[:, t:t + 1], e, m(L, "x_sel"))
                        dve.wait_ge(m(L, "x_xg"), b1 + j)
                        xe_out(2, m(L, "x_xe"), m(L, "x_xm"), b1 + j)
                        dve.wait_ge(m(L, "x_sg"), b1 + j)
                        hidden(2, m(L, "x_h"))
                        dve.wait_ge(m(L, "x_y"), b1 + j)
                        dve.wait_ge(m(L, "xdone"), b1 + j)
                        ye_out(2, m(L, "x_ye"))

            dve.wait_ge(m(L, "table"), 1)
            dve.wait_ge(m(L, "xdone"), 1)
            choose(0, ranks(0), 0, S("expert_sel"))
            choose(1, ranks(1), 1, S("expert_sel"))
            wait_expert(dve, L, "xg", 1)
            xe_out(0, S("expert_xe"), S("expert_xm"), NE * (L - 1) + 1)
            expert(0, 0, True, False)
            expert(1, 1, True, False)
            with dve.Fori(1, NE // 2 - 1) as i:
                for a in range(2):
                    expert(2 * i + a, a, True, False)
            expert(NE - 2, 0, False, False)
            expert(NE - 1, 1, False, True)

        def deepnorm(keys, s, k):
            for h in range(2):
                read(dve, ("gate", s, h))
            for t in range(NT):
                for h in range(2):
                    o = result(dve, keys(t, h))
                    tmp = SM[:, :, :].rearrange("p a b -> p (a b)")[:, 0:512]
                    drain(V.tensor_tensor(tmp, o, GB[:, 512 * h:512 * h + 512], ALU.mult), keys(t, h))
                    read(dve, keys(t, h))
                    v = X[:, t, 512 * h:512 * h + 512]
                    link(V.scalar_tensor_tensor(out=v, in0=v, scalar=ALPHA, in1=tmp, op0=ALU.mult, op1=ALU.add))
            rstd(moments(lambda t: X[:, t, :], D, EPS_LN, False))
            dve.wait_ge(S("gains_in"), 16 + 32 * k)
            for t in range(NT):
                v = X[:, t, :]
                link(V.tensor_scalar(v, v, MV[:, 0, t, 0:1], RS[:, 0, t:t + 1], ALU.subtract, ALU.mult))
                link(V.tensor_tensor(v, v, LNG[:, 0, :], ALU.mult))
                ins = V.tensor_tensor(v, v, LNG[:, 1, :], ALU.add)
                if t == 0:
                    link(ins)
            ins.then_inc(S("x_ready"), 1)
            dve.wait_ge(S("x_ready"), k + 1)

        def diag(s):
            dve.wait_ge(S("ada_set"), s + 1)
            V.tensor_tensor(GB[:, :].rearrange("p (c n) -> p c n", n=P), bc(ident, [KC, P], 1),
                            ADA[:, 24 * s + 16:24 * s + 24].unsqueeze(2).broadcast_to([P, KC, P]), ALU.mult).then_inc(S("diag"), 1)

        if NLAYER > 0:
            moe(0)
            residual(lambda t, h: ("y", 0, 2 * t + h))
            rstd(moments(lambda t: X[:, t, :], D, EPS_RMS, True))
            dve.wait_ge(S("gains_in"), 16)
            for t in range(NT):
                v = X[:, t, :]
                ins = V.scalar_tensor_tensor(out=v, in0=v, scalar=RS[:, 0, t:t + 1], in1=LNG[:, 0, :], op0=ALU.mult, op1=ALU.mult)
            ins.then_inc(S("x_ready"), 1)
            dve.wait_ge(S("x_ready"), 1)
        if ("sb", 0) in order:
            diag(0)
            turn_out("sbx", KC, lambda c: hT[:, c, :])

            def weights(h):
                dve.wait_ge(S("log1p"), 4)
                o = result(dve, ("z2", h))
                e = SE[:, h, :]
                link(V.scalar_tensor_tensor(out=e, in0=o[:, 0:384], scalar=0.0, in1=e, op0=ALU.max, op1=ALU.add))
                d = e.rearrange("p (b q) -> p b q", b=3)[:, 0:3:2, :]
                V.tensor_tensor(d, d, bc(cst(C_CAUSAL), [2, P], 1), ALU.mult).then_inc(S("sp"), 1)

            def values_out(h):
                o = result(dve, ("sv", h))
                r = half_rows(h)
                drain(V.tensor_copy(hT[r, h // 2, :], o[r, 0:SEQ]), ("sv", h))

            ada_sum(12)
            ada_sum(13)
            for h in range(16):
                weights(h)
                if h >= 2:
                    values_out(h - 2)
                if h % 5 == 0 and h > 0:
                    ada_sum(13 + h // 5)
            values_out(14)
            values_out(15)
            ada_sum(17)
            deepnorm(lambda t, h: ("sb_out", "o", t, h), 0, 1)
        if NLAYER > 1:
            diag(1)
            moe(1)
            deepnorm(lambda t, h: ("y", 1, 2 * t + h), 1, 2)
        if ("ret", 0) in order:
            turn_out("rx", KC, lambda c: hT[:, c, :])
            dve.wait_ge(S("cos_sin"), 1)
            for n, (raw, dst) in enumerate(((RQRAW, RQ), (RKRAW, RK))):
                for j in range(2):
                    for t in range(NT):
                        read(dve, (("ret", 2 * n + j), t))
                x = raw.rearrange("p t (h d) -> p t h d", d=P)
                y = dst.rearrange("p t (h d) -> p t h d", d=P)
                for t in range(NT):
                    cos, sin = (bc(CS2[:, i, t, :], [8, 64], 1) for i in range(2))
                    x1, x2 = x[:, t, :, 0:64], x[:, t, :, 64:128]
                    a1 = RT1[:, t, :].rearrange("p (h i) -> p h i", i=64)
                    a2 = RT2[:, t, :].rearrange("p (h i) -> p h i", i=64)
                    V.tensor_tensor(a1, x1, cos, ALU.mult)
                    link(V.tensor_tensor(a2, x2, sin, ALU.mult))
                    link(V.tensor_tensor(y[:, t, :, 0:64], a1, a2, ALU.subtract))
                    V.tensor_tensor(a1, x2, cos, ALU.mult)
                    link(V.tensor_tensor(a2, x1, sin, ALU.mult))
                    ins = V.tensor_tensor(y[:, t, :, 64:128], a1, a2, ALU.add)
                    if n == 1 and t == 1:
                        ins.then_inc(S("ret_roped"), 1)
                    else:
                        link(ins)
            turn_out("rq", KC, lambda c: RQT[:, c, :])
            turn_out("rk", KC, lambda c: RKT[:, c, :])
            diag(2)
            dve.wait_ge(S("decay_in"), 16)

            def decayed(h):
                if h >= 2:
                    result(dve, ("rv", h - 2))
                o = result(dve, ("rs", h))
                drain(V.tensor_tensor(SM[:, h % 2, :], o[:, 0:384], DM[:, 384 * h:384 * h + 384], ALU.mult), ("rs", h))

            def stats(h):
                o = result(dve, ("rv", h))
                return moments(lambda t: o[:, 256 * t:256 * t + 256], 256, EPS_LN, False, h % 2)

            def gated(h, k):
                rstd(k)
                for j in range(8, 12):
                    for t in range(NT):
                        read(dve, (("ret", j), t))
                o = result(dve, ("rv", h))
                for t in range(NT):
                    v = RG[:, t, 256 * h:256 * h + 256]
                    ins = V.scalar_tensor_tensor(out=v, in0=o[:, 256 * t:256 * t + 256], scalar=MV[:, h % 2, t, 0:1], in1=v, op0=ALU.subtract, op1=ALU.mult)
                drain(ins, ("rv", h))
                read(dve, ("rv", h))
                for t in range(NT):
                    v = RG[:, t, 256 * h:256 * h + 256]
                    ins = V.tensor_scalar(v, v, RS[:, h % 2, t:t + 1], None, ALU.mult)
                if h == 7:
                    ins.then_inc(S("ret_gated"), 1)

            decayed(0)
            k_ = {}
            for h in range(8):
                if h < 7:
                    decayed(h + 1)
                k_[h] = stats(h)
                if h >= 1:
                    gated(h - 1, k_[h - 1])
                if 1 <= h <= 6:
                    ada_sum(18 + h - 1)
            gated(7, k_[7])
            turn_out("ro", 16, lambda c: ROT[:, c, :])
            deepnorm(lambda t, h: ("ret_out", "o", t, h), 2, 3)
        if NLAYER > 2:
            diag(3)
            moe(2)
            deepnorm(lambda t, h: ("y", 2, 2 * t + h), 3, 4)
        if NLAYER == 0:
            V.tensor_copy(POSF[:, 0:1], POSF[:, 0:1]).then_inc(S("x_ready"), 1)

    @block.gpsimd
    def _(pool):
        nc.gpsimd.memset(NEGH[:, :], -0.5).then_inc(S("neg_half"), 1)
        pool.wait_ge(S("neg_half"), 1)
        pool.dma_start(LNG[:, 0, :], A["g_final"].partition_broadcast(P)).then_inc(S("gains_in"), 16)
        k = 0
        for n, (width, par) in enumerate(norms):
            pool.wait_ge(S("square"), n + 1)
            nc.gpsimd.tensor_tensor(RS[:, par, 0:width], MS[:, par, 0:width], NEGH[:, 0:width], ALU.pow).then_inc(S("rstd"), 1)
            if n + 1 in RELOADS:
                i = RELOADS.index(n + 1)
                pool.wait_ge(S("x_ready"), i + 1)
                g, b = A["ln_g_2"][i // 2, i % 2], A["ln_b_2"][i // 2, i % 2]
                pool.dma_start(LNG[:, 0, :], g.partition_broadcast(P)).then_inc(S("gains_in"), 16)
                pool.dma_start(LNG[:, 1, :], b.partition_broadcast(P)).then_inc(S("gains_in"), 16)
                if i == 0:
                    pool.dma_start(DM[:, :], A["decay"]).then_inc(S("decay_in"), 16)
        pool.wait_ge(S("gains_in"), 16)
    ctx.close()


RELOADS = [7, 8, 9, 18]

NAMES = ['x', 'mem', 'g_mix', 'w_in', 'g_q', 'g_k', 'w_att_out', 'sgu_ln_g', 'sgu_ln_b', 'w_s', 'b_s', 'w_sgu_out', 'w_out',
         'g_cross', 'g_mem', 'w_cq', 'w_ckv', 'w_co', 'g_moe', 'w_rg', 'b_rg', 'w_re', 'b_re', 'w_gate', 'w_up', 'w_down',
         'g_final', 'c_2', 'positions_2', 'ada_w_2', 'ada_b_2', 'ln_g_2', 'ln_b_2', 'sb_w_in_2', 'sb_w_out_2',
         'ret_w_in_2', 'ret_gn_g_2', 'ret_w_out_2', 'router_w_2', 'router_b_2', 'moe_w_gate_2', 'moe_w_up_2', 'moe_w_down_2']
STOP = None
FINAL = {None: 5, ('co',): 1, ('moe', 0): 1, ('sb_out',): 2, ('moe', 1): 3, ('ret_out',): 4}


def kernel(**inputs):
    import concourse.bacc as bacc
    from concourse.bass_utils import run_bass_kernel_spmd

    nc = bacc.Bacc("TRN2", target_bir_lowering=False, num_devices=1)
    arrays, A = {}, {}
    given = [(name, np.ascontiguousarray(inputs[name])) for name in NAMES] + [("cst", constants()), ("decay", decay_table())]
    for name, a in given:
        arrays[f"in_{name}"] = a
        A[name] = nc.dram_tensor(f"in_{name}", a.shape, mybir.dt.from_np(a.dtype), kind="ExternalInput").ap()
    out = nc.dram_tensor("out_x", (1, SEQ, D), F32, kind="ExternalOutput").ap()
    build(nc, A, out, STOP, FINAL[STOP])
    r = run_bass_kernel_spmd(nc, [arrays], core_ids=[0])
    return r.results[0]["out_x"]
```

```python
from contextlib import ExitStack

import concourse.bass as bass
import numpy as np
from concourse import mybir

F32 = mybir.dt.float32
F32R = mybir.dt.float32r
I32 = mybir.dt.int32
U32 = mybir.dt.uint32
ALU = mybir.AluOpType
ACT = mybir.ActivationFunctionType
AX = mybir.AxisListType.X

P = 128
SEQ = 256
NT = SEQ // P
D = 1024
KC = D // P
PAN = 4096
RING = 6
DRING = 3
ADA_PE = 12
QUARTERS = 4
CAP = 64
NE = 16
PER = 3
EPS_RMS = 1e-6
EPS_LN = 1e-5
ALPHA = 4.0 ** 0.25
ATT_SCALE = 64.0 ** -0.5
X_SCALE = 128.0 ** -0.5
BIG = 1e30

C_ID, C_NEGU, C_NEG1, C_CAUSAL, C_NEGMASK, C_PREFIX, C_ONES, C_SLOT = [i * P for i in range(8)]
C_ROPE = 8 * P
C_GRP = C_ROPE + 128
C_EXP = C_GRP + 16
C_OFF = C_EXP + 16
C_PICK = C_OFF + 3
C_INVF = C_PICK + 1
CST_COLS = C_INVF + 64


def constants():
    i = np.arange(P)
    c = np.zeros((P, CST_COLS), np.float32)
    c[:, C_ID:C_ID + P] = np.eye(P)
    c[:, C_NEGU:C_NEGU + P] = np.where(i[:, None] >= i[None, :], -1.0, 0.0)
    c[:, C_NEG1:C_NEG1 + P] = -1.0
    c[:, C_CAUSAL:C_CAUSAL + P] = i[:, None] < i[None, :]
    c[:, C_NEGMASK:C_NEGMASK + P] = np.where(i[:, None] < i[None, :], 0.0, -BIG)
    c[:, C_PREFIX:C_PREFIX + P] = i[:, None] < i[None, :]
    c[:, C_ONES:C_ONES + P] = 1.0
    c[:, C_SLOT:C_SLOT + P] = i[None, :] % CAP
    inv = (10000.0 ** (-np.arange(16, dtype=np.float32) / np.float32(16))).astype(np.float32)
    for t in range(NT):
        s = t * P + i
        ang = np.concatenate([(s // 64)[:, None].astype(np.float32) * inv, (s % 64)[:, None].astype(np.float32) * inv], 1)
        c[:, C_ROPE + 64 * t:C_ROPE + 64 * t + 32] = np.cos(ang)
        c[:, C_ROPE + 64 * t + 32:C_ROPE + 64 * t + 64] = np.sin(ang)
    c[:, C_GRP:C_GRP + 16] = np.arange(16) // 4
    c[:, C_EXP:C_EXP + 16] = np.arange(16)
    c[:, C_OFF:C_OFF + 3] = CAP * np.arange(1, 4)
    c[::32, C_PICK] = 1.0
    c[:, C_INVF:C_INVF + 64] = 1.0 / (np.float32(10000.0) ** (np.arange(0, 128, 2, dtype=np.float32) / np.float32(128)))
    return c


def decay_table():
    g = np.log(1.0 - np.exp2(-5.0 - np.arange(8.0)))
    m = np.arange(P)[:, None, None]
    n = np.arange(P)[None, None, :]
    lg = g[None, :, None]
    same = np.where(n >= m, np.exp(np.maximum(n - m, 0) * lg), 0.0)
    cross = np.exp((P - 1.0 - m) * lg) * np.exp((n + 1.0) * lg)
    return (np.concatenate([same, cross, same], 2) * 128.0 ** -0.5).astype(np.float32).reshape(P, 8 * 384)


def build(nc, A, out, stop, final_ready):
    ctx = ExitStack()

    def sb(name, shape, dt=F32):
        return ctx.enter_context(nc.sbuf_tensor(name, shape, dt))

    sems = {}

    def S(name):
        if name not in sems:
            sems[name] = ctx.enter_context(nc.semaphore(name))
        return sems[name]

    ring_lo = sb("ring_lo", [P, DRING, PAN])
    with nc.sbuf_tensor("ring_hi", [P, RING - DRING, PAN], F32) as ring_hi:
        pass
    WHI = sb("WHI", [P, QUARTERS, PAN // QUARTERS], F32R)
    WLO = sb("WLO", [P, QUARTERS, PAN // QUARTERS], F32R)
    HTH = sb("HTH", [P, KC, SEQ], F32R)
    HTL = sb("HTL", [P, KC, SEQ], F32R)

    def high(c):
        return HTH[:, c, :] if c < KC else ROH[:, c - KC, :]

    def low(c):
        return HTL[:, c, :] if c < KC else ROL[:, c - KC, :]

    def slot(r):
        return ring_lo[:, r, :] if r < DRING else ring_hi[:, r - DRING, :]

    X = sb("X", [P, NT, D])
    with nc.sbuf_tensor("hT", [P, KC, SEQ], F32) as hT:
        pass
    YLS = sb("YLS", [P, 3, 512], F32R)
    sb("hT_rest", [P, KC * SEQ - 3 * 512])
    ZR, ZT = 8960, 11264
    with nc.sbuf_tensor("Z", [P, 12288], F32) as Z:
        pass
    ROH, ROL = sb("ROH", [P, KC, SEQ], F32R), sb("ROL", [P, KC, SEQ], F32R)
    sb("Z_low", [P, ZR - 2 * KC * SEQ])
    SELTS = sb("SELTS", [P, 3, SEQ], F32R)
    YHS = sb("YHS", [P, 3, 512], F32R)
    sb("Z_high", [P, 12288 - ZT])
    DM = sb("DM", [P, 3072])
    LNG = sb("LNG", [P, 2, D])
    GB = sb("GB", [P, D])
    CST = sb("CST", [P, CST_COLS])
    VT = sb("VT", [P, 2, 96])
    ADA = sb("ADA", [P, 96])
    AROW = sb("AROW", [P, 2, 512])
    MASK = sb("MASK", [P, 2, P], F32R)
    UNREAD = sb("UNREAD", [P, 1])
    SILC = sb("SILC", [P, KC, 32])
    WST = sb("WST", [P, 4, P])
    WR1 = sb("WR1", [P, KC, 20])
    WR2 = sb("WR2", [P, KC, 16])
    BR1 = sb("BR1", [P, 20])
    BR2 = sb("BR2", [P, 16])
    GQK = sb("GQK", [P, 10, 64])
    SGB = GB[:, :].rearrange("p (k n) -> p k n", k=2)
    SM = sb("SM", [P, 2, 384])
    CS2 = sb("CS2", [P, 2, NT, 64])
    POS = sb("POS", [P, NT], I32)
    POSF = sb("POSF", [P, NT])
    ST = sb("ST", [P, 2, NT, 2, 6])
    MV = sb("MV", [P, 2, NT, 2])
    MS = sb("MS", [P, 2, 20])
    RS = sb("RS", [P, 2, 20])
    NEGH = sb("NEGH", [P, 20])
    SX = sb("SX", [P, 2, 3, NT])
    RTI = sb("RTI", [P, 2, NT, 8], U32)
    TBL = sb("TBL", [1, 3, 3, NE], I32)
    TBF = sb("TBF", [1, 8, NE])
    ps = ctx.enter_context(nc.psum_tensor("ps", [P, 8, 512], F32))

    def cst(at, n=P, rows=slice(0, P)):
        return CST[rows, at:at + n]

    ident = cst(C_ID)
    V_MIX, V_CROSS, V_MEM, V_MOE, V_C, V_GN, V_BS = 0, 8, 16, 24, 32, 40, 56

    filled = [S(f"filled{b}") for b in range(8)]
    drained = [S(f"drained{b}") for b in range(8)]
    uses = [0] * 8
    turn = {"A": 0, "B": 0}
    where = {}
    POOLS = {"A": [0, 1, 2, 3], "B": [4, 5, 6, 7]}

    def claim(pe, key, pool):
        b = POOLS[pool][turn[pool] % 4]
        turn[pool] += 1
        if uses[b]:
            pe.wait_ge(drained[b], uses[b])
        uses[b] += 1
        assert key not in where, key
        where[key] = (b, uses[b])
        return ps[:, b, :]

    def fill(ins, key):
        ins.then_inc(filled[where[key][0]], 1)

    def result(eng, key):
        b, k = where[key]
        eng.wait_ge(filled[b], k)
        return ps[:, b, :]

    def drain(ins, key):
        ins.then_inc(drained[where[key][0]], 1)

    def read(eng, key):
        b, k = where[key]
        eng.wait_ge(drained[b], k)

    def k8(w, c0, n=512):
        return w[:, c0:c0 + n].rearrange("(c p) n -> p c n", p=P), KC * n

    def k4(w, r0):
        return w[r0:r0 + 512, :].rearrange("(c p) n -> p c n", p=P), PAN

    ada = [A["ada_w_2"][s // 2, s % 2] for s in range(4)]
    w_in, w_ckv, sbw, rtw = A["w_in"][0], A["w_ckv"][0], A["sb_w_in_2"][0], A["ret_w_in_2"][0]
    stream = [(("ckv", j), k8(w_ckv, 512 * j)) for j in range(2)]
    IN = [("q", 0, 512), ("kv", 512, 256), ("su", 768, 512), ("sv", 1280, 512), ("ga0", 1792, 512),
          ("ga1", 2304, 512), ("gb0", 2816, 512), ("gb1", 3328, 512)]
    def ada_panels(ns):
        return [(("ada", n), k8(ada[n // 6], 512 * (n % 6))) for n in ns]

    ADA_AFTER = {("in", "gb1"): range(8), ("cq", 0): range(8, 12), ("sb", 1): (12,), ("sb", 2): (13,), ("sb", 3): (14,), ("sb", 4): (15,), ("sb", 5): (16, 17),
                 ("ret", 1): (18,), ("ret", 2): (19,), ("ret", 6): (20,), ("ret", 7): (21,), ("ret", 8): (22,), ("ret", 9): (23,)}
    stream += [(("in", n), k8(w_in, c0, w)) for n, c0, w in IN]
    stream += [(("att_out", 0), k4(A["w_att_out"][0], 0)), (("sgu_out", 0), k4(A["w_sgu_out"][0], 0))]
    stream += [(("w_out", j), k4(A["w_out"][0], 512 * j)) for j in range(2)]
    stream += [(("cq", 0), k8(A["w_cq"][0], 0)), (("co", 0), k4(A["w_co"][0], 0))]
    stream += [(("moe", 0), None)]
    stream += [(("sb", j), k8(sbw, 512 * j)) for j in range(6)]
    stream += [(("sb_out", j), k4(A["sb_w_out_2"][0], 512 * j)) for j in range(2)]
    stream += [(("moe", 1), None)]
    stream += [(("ret", j), k8(rtw, 512 * j)) for j in range(12)]
    stream += [(("ret_out", j), k4(A["ret_w_out_2"][0], 512 * j)) for j in range(4)]
    stream += [(("moe", 2), None)]
    MOE_W = [(A["w_gate"][0], A["w_up"][0], A["w_down"][0])] + [
        (A["moe_w_gate_2"][i], A["moe_w_up_2"][i], A["moe_w_down_2"][i]) for i in range(2)]
    stream = [x for key, src in stream for x in [(key, src)] + ada_panels(ADA_AFTER.get(key, ()))]
    if stop:
        last = max(i for i, (key, _) in enumerate(stream) if key[0] == stop[0] and (len(stop) == 1 or key[1] == stop[1]))
        stream = stream[:last + 1]
    DIRECT = ("ada",)
    place, count, user, turn_d = {}, [0] * RING, [None] * RING, 0
    split_no = {}
    last_split = None
    for key, src in stream:
        for j in range(1 if src else PER * NE):
            if src:
                r = turn_d % DRING
                turn_d += 1
            else:
                r = PER * (j // PER % 2) + j % PER
            count[r] += 16
            before = user[r]
            if not src and r >= DRING and j < 2 * PER:
                before = (last_split, 0)
            place[key, j] = (r, count[r], before)
            user[r] = (key, j)
        if src and key[0] not in DIRECT:
            split_no[key] = len(split_no)
            last_split = key
    split_keys = list(split_no)
    order = [key for key, _ in stream]
    progress = [0]
    taken = [key for key in order if key[0] != "ada" or key[1] < ADA_PE]
    freed_by, op_reads = {}, [0]
    landed = [S(f"landed{r}") for r in range(RING)]

    def panel(pe, key, n):
        assert taken[progress[0]] == key, (taken[progress[0]], key)
        progress[0] += 1
        r, landed_at, _ = place[key, 0]
        pe.wait_ge(landed[r], landed_at)
        w = stream[order.index(key)][1][1]
        return slot(r)[:, 0:w].rearrange("p (c n) -> p c n", n=n)

    def zv(at, *shape):
        v = Z[:, at:at + int(np.prod(shape))]
        if len(shape) == 2:
            return v.rearrange("p (a b) -> p a b", b=shape[1])
        return v

    MEM = zv(0, NT, D)
    MEMN = zv(2048, NT, D)
    WSR = zv(4096, 512)
    VROW = zv(5248, 2, P)
    ANG, KK, RR = zv(4608, 128), zv(4736, 2, 128), zv(4992, 2, 128)
    MKT = DM[:, 0:1024].rearrange("p (h m) -> p h m", h=4)
    MVV = DM[:, 1024:2048].rearrange("p (t n) -> p t n", t=NT)
    QK5 = zv(0, NT, 640)
    SU, SV = zv(1536, NT, 512), zv(2560, NT, 512)
    GA, GBT = zv(3584, NT, D), zv(5632, NT, D)
    R5 = zv(7680, NT, 640)
    KD = zv(8960, NT, 256)
    TMP = zv(9472, 2, 512)
    GQT, GKT, GV = zv(10496, 4, SEQ), zv(11520, 2, SEQ), zv(12032, NT, P)
    QR = R5
    CQT = zv(2048, 4, SEQ)
    prob_buf = {"g": [zv(9472 + 512 * i, NT, SEQ) for i in range(2)], "c": [zv(3072 + 512 * i, NT, SEQ) for i in range(2)]}
    probT_buf = {"g": [zv(512 * i, 512) for i in range(2)], "c": [zv(4096 + 512 * i, 512) for i in range(2)]}
    SQT, SKT, SBV, SE = zv(0, 8, SEQ), zv(2048, 8, SEQ), zv(4096, NT, D), zv(6144, 16, 384)
    RV, RG = zv(0, NT, 2048), zv(4096, NT, 2048)
    RQRAW, RKRAW = zv(0, NT, D), zv(2048, NT, D)
    RQ, RK = zv(4096, NT, D), zv(6144, NT, D)
    RQT, RKT = zv(8192, 8, SEQ), zv(10240, 8, SEQ)
    RT1, RT2 = zv(10240, NT, 512), zv(11264, NT, 512)

    XN = Z[:, 0:2048].rearrange("p (t d) -> p t d", t=NT)

    def mb(a, at, n):
        base = 2048 + 2304 * a + at
        return Z[:, base:base + n]

    SEL_ = [mb(a, 256, 256).rearrange("p (t s) -> p t s", t=NT) for a in range(3)]
    XE = [mb(a, 512, 512).rearrange("p (c s) -> p c s", s=CAP) for a in range(3)]
    SG = [mb(a, 1024, 512) for a in range(3)]
    HH = [mb(a, 1536, 512) for a in range(3)]
    HT = [mb(a, 2048, 256).rearrange("p (c s) -> p c s", s=CAP) for a in range(3)]
    SELT_ = [SELTS[:, a, :] for a in range(3)]
    WTOK, WSLOT = [mb(a, 0, NT) for a in range(3)], [mb(a, NT, 1) for a in range(3)]
    YH, YL = [YHS[:, a, :] for a in range(3)], [YLS[:, a, :] for a in range(3)]
    RT = Z[:, 11264:12288]
    RANK = RT[:, 0:32].rearrange("p (t e) -> p t e", t=NT)
    COMB = RT[:, 32:64].rearrange("p (t e) -> p t e", t=NT)
    SELT = RT[:, 64:96].rearrange("p (t e) -> p t e", t=NT)
    RKX = RT[:, 96:98]
    B_XG, B_TR, B_GU, B_Y = 4, 5, 6, 7

    def m(L, name):
        return S(f"m{L}_{name}")

    def wait_expert(eng, L, name, v):
        v = v + L * (NE - 1 if name == "scat" else NE)
        if not isinstance(v, int) or v > 0:
            eng.wait_ge(S("expert_" + name), v)

    block = ctx.enter_context(nc.Block())
    NLAYER = sum(1 for k in order if k[0] == "moe")

    @block.tensor
    def _(pe):
        def mm(o, l, r, start, stop):
            return nc.tensor.matmul(o, l, r, start=start, stop=stop, skip_group_check=True)

        def transposes(key, src, chunks):
            for j in range((chunks + 1) // 2):
                o = claim(pe, (key, j), "B")
                for c in (2 * j, 2 * j + 1):
                    if c < chunks:
                        for t in range(NT):
                            at = (c % 2) * SEQ + t * P
                            ins = nc.tensor.transpose(o[:, at:at + P], src(t, c), ident)
                fill(ins, (key, j))

        def turned(key, chunks):
            for j in range((chunks + 1) // 2):
                read(pe, (key, j))

        def quarters(key, n):
            assert taken[progress[0]] == key, (taken[progress[0]], key)
            progress[0] += 1
            size = stream[order.index(key)][1][1] // QUARTERS
            for q in range(QUARTERS):
                pe.wait_ge(S("lo_split"), QUARTERS * split_no[key] + q + 1)
                hi, lo = (w[:, q, 0:size].rearrange("p (c n) -> p c n", n=n) for w in (WHI, WLO))
                yield q, q * size // n, hi, lo

        def quarter_read(ins):
            ins.then_inc(S("quarter_read"), 1)

        def three(o, l, lh, ll, r, rh, rl, start, stop):
            mm(o, lh[l], rh[r], start, False)
            mm(o, lh[l], rl[r], False, False)
            return mm(o, ll[l], rh[r], False, stop)

        def project(key, n=512):
            banks = [claim(pe, (key, t), "A") for t in range(NT)]
            for q, c0, hi, lo in quarters(key, n):
                k = KC // QUARTERS
                for t in range(NT):
                    for c in range(k):
                        ins = three(banks[t][:, 0:n], (slice(None), c0 + c, slice(t * P, (t + 1) * P)), HTH, HTL,
                                    (slice(None), c, slice(None)), hi, lo, c0 + c == 0, c0 + c == KC - 1)
                    if q == QUARTERS - 1:
                        fill(ins, (key, t))
                if q < QUARTERS - 1:
                    quarter_read(ins)
            released(key, (key, NT - 1))

        def project_T(key):
            banks = [claim(pe, (key, f), "A") for f in range(2)]
            for q, c0, hi, lo in quarters(key, 512):
                for f in range(2):
                    for g in range(2):
                        col = (2 * f + g) * P
                        for c in range(KC // QUARTERS):
                            ins = three(banks[f][:, g * SEQ:(g + 1) * SEQ], (slice(None), c, slice(col, col + P)), hi, lo,
                                        (slice(None), c0 + c, slice(None)), HTH, HTL, c0 + c == 0 and g == 0, c0 + c == KC - 1)
                    if q == QUARTERS - 1:
                        fill(ins, (key, f))
                if q < QUARTERS - 1:
                    quarter_read(ins)
            released(key, (key, 1))

        def out_project(key, panels, at=0):
            banks = {(t, h): claim(pe, (key, "o", t, h), "A") for t in range(NT) for h in range(2)}
            for j in range(panels):
                for q, c0, hi, lo in quarters((key, j), D):
                    first, last = j == 0 and q == 0, j == panels - 1 and q == QUARTERS - 1
                    for t in range(NT):
                        for h in range(2):
                            c = at + 4 * j + c0
                            ins = three(banks[t, h], (slice(None), slice(t * P, (t + 1) * P)), high(c), low(c),
                                        (slice(None), 0, slice(h * 512, (h + 1) * 512)), hi, lo, first, last)
                            if last:
                                fill(ins, (key, "o", t, h))
                    if q < QUARTERS - 1:
                        quarter_read(ins)
                    elif not last:
                        out_read(key, j, ins)
                if j == panels - 1:
                    released((key, j), (key, "o", NT - 1, 1))

        def out_read(key, j, ins):
            op_reads[0] += 1
            ins.then_inc(S("out_panel_read"), 1)
            freed_by[(key, j)] = (S("out_panel_read"), op_reads[0])

        def released(key, last):
            b, k = where[last]
            freed_by[key] = (filled[b], k)

        pending = []

        def ada_flush():
            if pending:
                n = pending.pop()
                read(pe, ("ada", n))
                o = claim(pe, ("adac", n), "A")
                for f in range(4):
                    ins = mm(o[:, f:f + 1], AROW[:, 0, f * P:(f + 1) * P], cst(C_PICK, 1), True, True)
                fill(ins, ("adac", n))

        def ada_panel(n):
            ada_flush()
            w = panel(pe, ("ada", n), 512)
            if n == 0:
                pe.wait_ge(S("silu_c"), 1)
            o = claim(pe, ("ada", n), "A")
            for c in range(KC):
                g = 32 * (c % 4)
                ins = mm(o[g:g + 32, :], SILC[:, c, :], w[:, c, :], c < 4, c >= 4)
            fill(ins, ("ada", n))
            released(("ada", n), ("ada", n))
            pending.append(n)

        def ada_turn(n):
            pe.wait_ge(S("ada_acc"), n + 1 - ADA_PE)
            o = claim(pe, ("adac", n), "B")
            for f in range(4):
                ins = mm(o[:, f:f + 1], AROW[:, n % 2, f * P:(f + 1) * P], cst(C_ONES, 1), True, True)
            fill(ins, ("adac", n))

        def keep_warm(n):
            b = POOLS["B"][turn["B"] % 4]
            if uses[b]:
                pe.wait_ge(drained[b], uses[b])
            for _ in range(n):
                mm(ps[:, b, :], ident, CST[:, 0:512], True, True)

        pe.wait_ge(S("cst_in"), 16)
        pe.wait_ge(S("vec_in"), 16 * 8)
        for i in range(2):
            o = claim(pe, ("vec", i), "B")
            r = (60, 96)[i]
            fill(nc.tensor.transpose(o[:, 0:r], VROW[0:r, i, :], CST[0:r, C_ID:C_ID + r]), ("vec", i))

        mn = Z[:, 2048:4096].rearrange("p (t d) -> p t d", t=NT)
        pe.wait_ge(S("xn_ready"), 1)
        transposes("mem", lambda t, c: mn[:, t, c * P:(c + 1) * P], KC)
        keep_warm(4)
        turned("mem", KC)
        project_T(("ckv", 0))
        project(("ckv", 1))

        pe.wait_ge(S("xn_ready"), 2)
        transposes("x", lambda t, c: XN[:, t, c * P:(c + 1) * P], KC)
        keep_warm(3)
        turned("x", KC)
        pe.wait_ge(S("ws_in"), 16)
        o = claim(pe, ("ws", 0), "B")
        for g in range(4):
            ins = nc.tensor.transpose(o[:, g * P:(g + 1) * P], Z[:, 4096 + g * P:4096 + (g + 1) * P], ident)
        fill(ins, ("ws", 0))
        for nme, _, w in IN:
            project(("in", nme), w)

        def attention(tag, heads, q_at, k_at, v_at, half, fillers):
            def scores(h):
                o = claim(pe, (tag, "s", h), "B")
                for t in range(NT):
                    ins = mm(o[:, t * SEQ:(t + 1) * SEQ], q_at(h)[:, t * P:(t + 1) * P], k_at(h), t == 0, t == NT - 1)
                fill(ins, (tag, "s", h))

            def turn_probs(h):
                pe.wait_ge(S(f"{tag}_probs"), h + 1)
                o = claim(pe, (tag, "p", h), "B")
                pr = prob_buf[tag][h % 2]
                for c in range(2):
                    for t in range(NT):
                        ins = nc.tensor.transpose(o[:, c * SEQ + t * P:c * SEQ + (t + 1) * P],
                                                  pr[:, t, c * P:(c + 1) * P], ident)
                fill(ins, (tag, "p", h))

            def values(h):
                read(pe, (tag, "p", h))
                o = claim(pe, (tag, "v", h), "A")
                pt = probT_buf[tag][h % 2]
                rows = slice(64 * (h % 2), 64 * (h % 2) + 64) if half else slice(0, P)
                for c in range(2):
                    ins = mm(o[rows, 0:SEQ], v_at(h, c), pt[:, c * SEQ:(c + 1) * SEQ], c == 0, c == 1)
                fill(ins, (tag, "v", h))

            scores(0)
            for h in range(heads):
                if h + 1 < heads:
                    scores(h + 1)
                if h < len(fillers):
                    ada_panel(fillers[h])
                turn_probs(h)
                if h >= 1:
                    values(h - 1)
            values(heads - 1)
            ada_flush()

        pe.wait_ge(S("qk_roped"), 1)
        transposes("gq", lambda t, c: QR[:, t, c * P:(c + 1) * P], 4)
        transposes("gk", lambda t, c: KD[:, t, c * P:(c + 1) * P], 2)
        turned("gq", 4)
        turned("gk", 2)
        for t in range(NT):
            read(pe, (("in", "kv"), t))
        def half_rows(h):
            return slice(64 * (h % 2), 64 * (h % 2) + 64)
        attention("g", 8, lambda h: GQT[half_rows(h), h // 2, :], lambda h: GKT[half_rows(h), h // 4, :],
                  lambda h, c: GV[:, c, 64 * (h // 4):64 * (h // 4) + 64], True, list(range(8)))

        read(pe, ("ws", 0))
        for t in range(NT):
            pe.wait_ge(S("sv_normed"), t + 1)
            o = claim(pe, ("sgu", t), "A")
            for g in range(4):
                ins = mm(o[:, g * P:(g + 1) * P], WST[:, g, :], SV[:, t, g * P:(g + 1) * P], True, True)
            fill(ins, ("sgu", t))
        for t in range(NT):
            read(pe, ("sgu", t))
        transposes("sg", lambda t, c: SU[:, t, c * P:(c + 1) * P], 4)
        for h in range(8):
            read(pe, ("g", "v", h))
        out_project("att_out", 1)
        turned("sg", 4)
        out_project("sgu_out", 1, 4)
        pe.wait_ge(S("merged"), 4)
        transposes("mg", lambda t, c: GA[:, t, c * P:(c + 1) * P], KC)
        turned("mg", KC)
        out_project("w_out", 2)
        keep_warm(7)

        pe.wait_ge(S("xn_ready"), 3)
        transposes("xc", lambda t, c: XN[:, t, c * P:(c + 1) * P], KC)
        keep_warm(2)
        turned("xc", KC)
        project_T(("cq", 0))
        for f in range(2):
            read(pe, (("cq", 0), f))
            read(pe, (("ckv", 0), f))
        for t in range(NT):
            read(pe, (("ckv", 1), t))
        attention("c", 4, lambda h: CQT[:, h, :], lambda h: MKT[:, h, :],
                  lambda h, c: MVV[:, c, h * P:(h + 1) * P], False, list(range(8, 12)))
        for h in range(4):
            read(pe, ("c", "v", h))
        out_project("co", 1)
        keep_warm(6)

        def gate_rows(s):
            pe.wait_ge(S("diag"), s + 1)
            for h in range(2):
                o = claim(pe, ("gate", s, h), "B")
                fill(mm(o, cst(C_ONES), GB[:, h * 512:(h + 1) * 512], True, True), ("gate", s, h))

        def moe(L):
            src = XN if L == 0 else X
            wr, nr = (WR1, 20) if L == 0 else (WR2, 16)
            if L == 0:
                pe.wait_ge(S("xn_ready"), 4)
            else:
                pe.wait_ge(S("x_ready"), 2 * L)
            transposes(("moe", L), lambda t, c: src[:, t, c * P:(c + 1) * P], KC)
            turned(("moe", L), KC)
            o = claim(pe, ("route", L), "B")
            for t in range(NT):
                for c in range(KC):
                    ins = mm(o[:, 32 * t:32 * t + nr], hT[:, c, t * P:(t + 1) * P], wr[:, c, :], c == 0, c == KC - 1)
            fill(ins, ("route", L))
            acc = [claim(pe, ("y", L, i), "A") for i in range(4)]
            pe.wait_ge(m(L, "zero"), 1)
            if L:
                gate_rows(2 * L - 1)
            for i in list(range(4)) * (2 if L else 4):
                ins = mm(acc[i], YH[0][:, 0:P], YH[0], True, False)
            ins.then_inc(m(L, "xdone"), 1)
            mm(acc[3], YH[0][:, 0:P], YH[0], True, False).then_inc(m(L, "x_gu"), 1)
            pe.wait_ge(m(L, "chosen"), 1)
            o = claim(pe, ("rank", L), "B")
            mm(o[:, 0:16], cst(C_PREFIX), SELT[:, 0, :], True, True)
            mm(o[:, 16:32], cst(C_PREFIX), SELT[:, 1, :], True, False)
            mm(o[:, 16:32], cst(C_ONES), SELT[:, 0, :], False, True)
            mm(o[:, 32:48], cst(C_ONES), SELT[:, 0, :], True, False)
            fill(mm(o[:, 32:48], cst(C_ONES), SELT[:, 1, :], False, True), ("rank", L))
            progress[0] += 1
            for b in range(4, 8):
                pe.wait_ge(drained[b], uses[b])

            def gather(a, done):
                for c in range(KC):
                    for t in range(NT):
                        mm(ps[:, B_XG, c * CAP:(c + 1) * CAP], src[:, t, c * P:(c + 1) * P], SEL_[a][:, t, 0:CAP],
                           t == 0, t == NT - 1)
                for t in range(NT):
                    ins = nc.tensor.transpose(ps[:, B_TR, t * P:(t + 1) * P], SEL_[a][:, t, :], ident)
                for t in range(NT):
                    ins = mm(ps[:, B_TR, SEQ:SEQ + 1], SEL_[a][:, t, :], WTOK[a][:, t:t + 1], t == 0, t == NT - 1)
                ins.then_inc(done, 1)

            def gate_up(a, wg, wu, done):
                for c in range(KC):
                    mm(ps[0:CAP, B_GU, :], XE[a][:, c, :], wg[:, c, :], c == 0, c == KC - 1)
                    ins = mm(ps[CAP:P, B_GU, :], XE[a][:, c, :], wu[:, c, :], c == 0, c == KC - 1)
                ins.then_inc(done, 1)

            def turn_h(a, done):
                for c in range(4):
                    ins = mm(ps[:, B_GU, c * CAP:(c + 1) * CAP],
                             HH[a][CAP:P, c * P:(c + 1) * P], CST[CAP:P, C_ID + CAP:C_ID + P], True, True)
                ins.then_inc(done, 1)

            def down(a, wd, done):
                for c in range(4):
                    mm(ps[0:CAP, B_Y, :], HT[a][:, c, :], wd[:, c, 0:512], c == 0, c == 3)
                    ins = mm(ps[CAP:P, B_Y, :], HT[a][:, c, :], wd[:, c, 512:1024], c == 0, c == 3)
                ins.then_inc(done, 1)

            def scatter(a, last):
                for t in range(NT):
                    for y in (YH, YL):
                        for h in range(2):
                            r = slice(CAP * h, CAP * (h + 1))
                            ins = mm(acc[2 * t + h], SELT_[a][r, t * P:(t + 1) * P], y[a][r, :], False, last and y is YL)
                            if last and y is YL:
                                fill(ins, ("y", L, 2 * t + h))
                return ins

            def expert(e, i, a, first, final):
                s = [place[("moe", L), PER * a + j][0] for j in range(PER)]
                at = [place[("moe", L), PER * a + j][1] for j in range(PER)]
                wg = slot(s[0]).rearrange("p (c n) -> p c n", n=512)
                wu = slot(s[1]).rearrange("p (c n) -> p c n", n=512)
                wd = slot(s[2]).rearrange("p (c n) -> p c n", n=D)
                wait_expert(pe, L, "xe", e + 1)
                wait_expert(pe, L, "h", e)
                for j in range(2):
                    pe.wait_ge(landed[s[j]], 16 * i + at[j])
                gate_up(a, wg, wu, S("expert_gu"))
                if not first:
                    wait_expert(pe, L, "ye", e)
                    wait_expert(pe, L, "swt", e)
                    scatter(1 - a, False).then_inc(S("expert_scat"), 1)
                wait_expert(pe, L, "h", e + 1)
                wait_expert(pe, L, "ht", e)
                turn_h(a, S("expert_htp"))
                if not final:
                    wait_expert(pe, L, "sel", e + 2)
                    wait_expert(pe, L, "swt", e + 1)
                    gather(1 - a, S("expert_xg"))
                wait_expert(pe, L, "ht", e + 1)
                pe.wait_ge(landed[s[2]], 16 * i + at[2])
                down(a, wd, S("expert_y"))
                nb = pe.value_load(TBL[0:1, L, 0, bass.ds(e, 1)], min_val=0, max_val=3)
                b1 = pe.value_load(TBL[0:1, L, 1, bass.ds(e, 1)], min_val=1, max_val=48)
                with pe.If(nb > 0):
                    with pe.Fori(0, nb) as j:
                        if not final:
                            wait_expert(pe, L, "xe", e + 2)
                            wait_expert(pe, L, "swt", e + 2)
                        pe.wait_ge(m(L, "x_sel"), b1 + j)
                        gather(2, m(L, "x_xg"))
                        pe.wait_ge(m(L, "x_xe"), b1 + j)
                        gate_up(2, wg, wu, m(L, "x_gu"))
                        pe.wait_ge(m(L, "x_h"), b1 + j)
                        turn_h(2, m(L, "x_htp"))
                        pe.wait_ge(m(L, "x_ht"), b1 + j)
                        wait_expert(pe, L, "ye", e + 1)
                        down(2, wd, m(L, "x_y"))
                        pe.wait_ge(m(L, "x_swt"), b1 + j)
                        pe.wait_ge(m(L, "x_ye"), b1 + j)
                        scatter(2, False).then_inc(m(L, "xdone"), 1)

            wait_expert(pe, L, "sel", 1)
            gather(0, S("expert_xg"))
            pe.wait_ge(m(L, "table"), 1)
            expert(0, 0, 0, True, False)
            expert(1, 0, 1, False, False)
            with pe.Fori(1, NE // 2 - 1) as i:
                for a in range(2):
                    expert(2 * i + a, i, a, False, False)
            expert(NE - 2, NE // 2 - 1, 0, False, False)
            expert(NE - 1, NE // 2 - 1, 1, False, True)
            wait_expert(pe, L, "ye", NE)
            wait_expert(pe, L, "swt", NE)
            scatter(1, True)
            keep_warm(8 if L == 0 else 16 if L == 1 else 0)

        if NLAYER > 0:
            moe(0)

        if ("sb", 0) in order:
            pe.wait_ge(S("x_ready"), 1)
            transposes("sbx", lambda t, c: X[:, t, c * P:(c + 1) * P], KC)
            keep_warm(4)
            turned("sbx", KC)
            for j in range(4):
                project_T(("sb", j))
                if j >= 2:
                    ada_turn(10 + j)
            for j in range(4, 6):
                project(("sb", j))
                ada_turn(10 + j)
            for j in range(4):
                for f in range(2):
                    read(pe, (("sb", j), f))
            gate_rows(0)

            def logits(key, h, pool, stop):
                o = claim(pe, key, pool)
                r = half_rows(h)
                mm(o[:, 0:256], SKT[r, h // 2, 0:P], SQT[r, h // 2, :], True, stop)
                fill(mm(o[:, 256:384], SKT[r, h // 2, P:SEQ], SQT[r, h // 2, P:SEQ], False, stop), key)

            for h in range(16):
                logits(("z1", h), h, "B", True)
                if h in (7, 11):
                    ada_turn(15 + h // 4)
            for j in range(4, 6):
                for t in range(NT):
                    read(pe, (("sb", j), t))

            def accumulate(h):
                pe.wait_ge(S("sp"), h + 1)
                o = ps[:, where[("z2", h)][0], :]
                e = SE[:, h, :]
                mm(o[:, 0:256], cst(C_NEGU), e[:, 0:256], False, False)
                mm(o[:, 256:384], cst(C_NEGU), e[:, 256:384], False, False)
                mm(o[:, 128:256], cst(C_NEG1), e[:, 256:384], False, False)
                mm(o[:, 0:128], MASK[:, 0, :], MASK[:, 1, :], False, False)
                mm(o[:, 256:384], MASK[:, 0, :], MASK[:, 1, :], False, True).then_inc(S("logit"), 1)

            def sb_values(h):
                read(pe, ("z2", h))
                o = claim(pe, ("sv", h), "A")
                r = half_rows(h)
                mm(o[r, 0:256], SBV[:, 0, 64 * h:64 * h + 64], SE[:, h, 0:256], True, False)
                fill(mm(o[r, 128:256], SBV[:, 1, 64 * h:64 * h + 64], SE[:, h, 256:384], False, True), ("sv", h))

            pe.wait_ge(S("mask_ready"), 1)
            logits(("z2", 0), 0, "B", False)
            logits(("z2", 1), 1, "B", False)
            for h in range(16):
                if h + 2 < 16:
                    logits(("z2", h + 2), h + 2, "B", False)
                accumulate(h)
                if h >= 1:
                    sb_values(h - 1)
            sb_values(15)
            for h in range(16):
                read(pe, ("sv", h))
            out_project("sb_out", 2)
            keep_warm(16)
        if NLAYER > 1:
            moe(1)

        if ("ret", 0) in order:
            pe.wait_ge(S("x_ready"), 3)
            transposes("rx", lambda t, c: X[:, t, c * P:(c + 1) * P], KC)
            keep_warm(4)
            turned("rx", KC)
            for j in range(6):
                project(("ret", j))
                if j in (1, 3):
                    ada_turn(18 + j // 2)
            pe.wait_ge(S("ret_roped"), 1)
            transposes("rq", lambda t, c: RQ[:, t, c * P:(c + 1) * P], KC)
            transposes("rk", lambda t, c: RK[:, t, c * P:(c + 1) * P], KC)
            ada_turn(20)
            for j in range(6, 12):
                project(("ret", j))
                if 7 <= j <= 9:
                    ada_turn(14 + j)
            turned("rq", KC)
            turned("rk", KC)
            gate_rows(2)
            for j in range(4, 8):
                for t in range(NT):
                    read(pe, (("ret", j), t))

            def ret_scores(h):
                o = claim(pe, ("rs", h), "B")
                mm(o[:, 0:256], RKT[:, h, 0:P], RQT[:, h, :], True, False)
                fill(mm(o[:, 256:384], RKT[:, h, P:SEQ], RQT[:, h, P:SEQ], False, True), ("rs", h))

            def ret_values(h):
                read(pe, ("rs", h))
                o = claim(pe, ("rv", h), "A")
                s = SM[:, h % 2, :]
                mm(o[:, 0:256], s[:, 0:128], RV[:, 0, 256 * h:256 * h + 256], True, True)
                mm(o[:, 256:512], s[:, 128:256], RV[:, 0, 256 * h:256 * h + 256], True, False)
                fill(mm(o[:, 256:512], s[:, 256:384], RV[:, 1, 256 * h:256 * h + 256], False, True), ("rv", h))

            ret_scores(0)
            for h in range(8):
                if h < 7:
                    ret_scores(h + 1)
                ret_values(h)
            for h in range(8):
                read(pe, ("rv", h))
            pe.wait_ge(S("ret_gated"), 1)
            transposes("ro", lambda t, c: RG[:, t, c * P:(c + 1) * P], 16)
            turned("ro", 16)
            out_project("ret_out", 4)
            keep_warm(14)
        if NLAYER > 2:
            moe(2)
        if stop is None:
            assert progress[0] == len(taken)

    @block.sync
    def _(sp):
        blocks_done = [None]

        def wait_expert_read(L, e, j):
            if j == 0:
                sp.wait_ge(m(L, "table"), 1)
                blocks_done[0] = sp.value_load(TBL[0:1, L, 2, bass.ds(e, 1)], min_val=1, max_val=48)
            done = blocks_done[0]
            wait_expert(sp, L, "gu" if j < 2 else "y", e + 1)
            sp.wait_ge(m(L, "x_gu" if j < 2 else "xdone"), done)

        def wait_slot(key, j):
            before = place[key, j][2]
            if before is None:
                return
            old, k = before
            if old[0] == "moe":
                wait_expert_read(old[1], k // PER, k % PER)
            elif old[0] == "ada" and old[1] >= ADA_PE:
                sp.wait_ge(S("ada_acc"), old[1] + 1 - ADA_PE)
            elif old in split_no and place[key, j][0] < DRING:
                sp.wait_ge(S("lo_split"), QUARTERS * (split_no[old] + 1))
            else:
                sp.wait_ge(*freed_by[old])

        def load(r, src, size):
            sp.dma_start(slot(r)[:, 0:size].rearrange("p (c n) -> p c n", n=src.shape[2]), src).then_inc(landed[r], 16)

        def load_expert(L, e, r, j):
            w = MOE_W[L][j][bass.ds(e, 1)]
            load(r, w.rearrange("o (c p) n -> p (o c) n", p=P), PAN)

        sp.dma_start(MEM, A["mem"][0].rearrange("(t p) d -> p t d", p=P)).then_inc(S("mem_in"), 16)
        sp.dma_start(CST[:, :], A["cst"]).then_inc(S("cst_in"), 16)
        sp.wait_ge(S("vec_in"), 16 * 8)
        for key, src in stream:
            if key == ("ckv", 1):
                sp.dma_start(X[:, :, :], A["x"][0].rearrange("(t p) d -> p t d", p=P)).then_inc(S("x_in"), 16)
            if src:
                wait_slot(key, 0)
                load(place[key, 0][0], *src)
                continue
            L = key[1]
            for e in range(2):
                for j in range(PER):
                    wait_slot(key, PER * e + j)
                    load_expert(L, e, PER * e + j, j)
            with sp.Fori(1, NE // 2) as i:
                for a in range(2):
                    for j in range(PER):
                        wait_expert_read(L, 2 * i + (a - 2), j)
                        load_expert(L, 2 * i + a, PER * a + j, j)
        sp.wait_ge(S("x_ready"), final_ready)
        sp.dma_start(out.rearrange("o (t p) d -> p (o t) d", p=P), X[:, :, :]).then_inc(S("stored"), 16)
        sp.wait_ge(S("stored"), 16)

    def bc(ap, shape, *axes):
        for a in axes:
            ap = ap.unsqueeze(a)
        return ap.broadcast_to([P] + list(shape))

    TURN = {
        "mem": (lambda c: VT[:, 0, V_MEM + c:V_MEM + c + 1], None), "x": (lambda c: VT[:, 0, V_MIX + c:V_MIX + c + 1], None),
        "xc": (lambda c: VT[:, 0, V_CROSS + c:V_CROSS + c + 1], None),
        ("moe", 0): (lambda c: VT[:, 0, V_MOE + c:V_MOE + c + 1], None),
        "ro": (lambda c: VT[:, 0, V_GN + c:V_GN + c + 1], None),
    }
    for tag, s in (("sbx", 0), (("moe", 1), 1), ("rx", 2), (("moe", 2), 3)):
        TURN[tag] = ((lambda s: lambda c: ADA[:, 24 * s + 8 + c:24 * s + 9 + c])(s), (lambda s: lambda c: ADA[:, 24 * s + c:24 * s + c + 1])(s))

    @block.scalar
    def _(act):
        Copy = ACT.Copy
        rows = [(A["g_mix"], V_MIX, 8), (A["g_cross"], V_CROSS, 8), (A["g_mem"], V_MEM, 8), (A["g_moe"], V_MOE, 8),
                (A["c_2"], V_C, 8), (A["ret_gn_g_2"], V_GN, 16)]
        for v, r, k in rows:
            nc.scalar.dma_start(VROW[r:r + k, 0, :], v.rearrange("o (k p) -> (o k) p", p=P)).then_inc(S("vec_in"), 16)
        nc.scalar.dma_start(VROW[V_BS:V_BS + 4, 0, :], A["b_s"][0]).then_inc(S("vec_in"), 16)
        nc.scalar.dma_start(VROW[0:96, 1, :], A["ada_b_2"].rearrange("a b (k p) -> (a b k) p", p=P)).then_inc(S("vec_in"), 16)
        nc.scalar.dma_start(WSR.rearrange("p (g q) -> p g q", g=4), A["w_s"][0].rearrange("g p q -> p g q")).then_inc(S("ws_in"), 16)
        nc.scalar.dma_start(POS[:, :], A["positions_2"][0].rearrange("(t p) -> p t", p=P), allow_slow_non_contiguous=True).then_inc(S("pos_in"), 16)
        small = [(GQK[:, 0:8, :], A["g_q"].unsqueeze(0).broadcast_to([P, 8, 64])), (GQK[:, 8:10, :], A["g_k"].unsqueeze(0).broadcast_to([P, 2, 64])),
                 (SGB[:, 0, :], A["sgu_ln_g"][0].partition_broadcast(P)), (SGB[:, 1, :], A["sgu_ln_b"][0].partition_broadcast(P)),
                 (WR1[:, :, 0:4], A["w_rg"][0].rearrange("(c p) n -> p c n", p=P)), (WR1[:, :, 4:20], A["w_re"][0].rearrange("(c p) n -> p c n", p=P)),
                 (WR2[:, :, :], A["router_w_2"].rearrange("(c p) n -> p c n", p=P)),
                 (BR1[:, 0:4], A["b_rg"][0].partition_broadcast(P)), (BR1[:, 4:20], A["b_re"][0].partition_broadcast(P)),
                 (BR2[:, :], A["router_b_2"].partition_broadcast(P))]
        def turn_out(key, chunks, dest):
            scale, shift = TURN.get(key, (None, None))
            for j in range(0, (chunks + 1) // 2, 2):
                o = result(act, (key, j))
                for c in (2 * j, 2 * j + 1):
                    i = o[:, (c % 2) * SEQ:(c % 2) * SEQ + SEQ]
                    if shift:
                        ins = nc.scalar.activation(dest(c), i, ACT.Identity, scale=scale(c), bias=shift(c))
                    elif scale:
                        ins = nc.scalar.activation(dest(c), i, Copy, scale=scale(c))
                    else:
                        ins = nc.scalar.activation(dest(c), i, Copy)
                drain(ins, (key, j))

        splits = [0]

        def split_next(key):
            n = splits[0]
            assert split_keys[n] == key, (key, split_keys[n])
            splits[0] += 1
            r, landed_at, _ = place[key, 0]
            act.wait_ge(landed[r], landed_at)
            size = stream[order.index(key)][1][1] // QUARTERS
            for q in range(QUARTERS):
                if n and q < QUARTERS - 1:
                    act.wait_ge(S("quarter_read"), (QUARTERS - 1) * (n - 1) + q + 1)
                elif n:
                    act.wait_ge(*freed_by[split_keys[n - 1]])
                nc.scalar.activation(WHI[:, q, 0:size], slot(r)[:, q * size:(q + 1) * size], Copy).then_inc(S("hi_split"), 1)

        def turn_split(key, chunks, at=0):
            scale, shift = TURN.get(key, (None, None))
            for j in range((chunks + 1) // 2):
                o = result(act, (key, j))
                for c in (2 * j, 2 * j + 1):
                    i = o[:, (c % 2) * SEQ:(c % 2) * SEQ + SEQ]
                    if shift:
                        ins = nc.scalar.activation(high(at + c), i, ACT.Identity, scale=scale(c), bias=shift(c))
                    elif scale:
                        ins = nc.scalar.activation(high(at + c), i, Copy, scale=scale(c))
                    else:
                        ins = nc.scalar.activation(high(at + c), i, Copy)
                ins.then_inc(S("turned_hi"), 1)

        def move(key, dst, src=slice(0, 512), func=Copy, **k):
            o = result(act, key)
            drain(nc.scalar.activation(dst, o[:, src], func, **k), key)

        def load_table(func):
            nc.scalar.activation(UNREAD[:, :], CST[:, 0:1], func)

        def halves(v):
            return v.rearrange("p a b -> p (a b)")

        act.wait_ge(S("cst_in"), 16)
        read(act, ("vec", 0))
        turn_split("mem", KC)
        split_next(("ckv", 0))
        nc.scalar.activation(MASK[:, 0, :], ident, Copy)
        nc.scalar.activation(MASK[:, 1, :], cst(C_NEGMASK), Copy).then_inc(S("mask_ready"), 1)
        nc.scalar.activation(SILC[:, :, :], bc(VT[:, 0, V_C:V_C + 8], [8, 32], 2), ACT.Silu).then_inc(S("silu_c"), 1)
        for dst, src in small:
            nc.scalar.dma_start(dst, src).then_inc(S("small_in"), 16)
        split_next(("ckv", 1))
        for f in range(2):
            move((("ckv", 0), f), halves(MKT[:, 2 * f:2 * f + 2, :]))
        split_next(("in", "q"))
        for t in range(NT):
            move((("ckv", 1), t), MVV[:, t, :])
        turn_split("x", KC)
        split_next(("in", "kv"))
        act.wait_ge(S("angles"), 1)
        nc.scalar.activation(CS2[:, :, :, :].rearrange("p a t i -> p a (t i)"), RR, ACT.Sin).then_inc(S("cos_sin"), 1)
        for t in range(NT):
            move((("in", "q"), t), QK5[:, t, 0:512])
        split_next(("in", "su"))
        for t in range(NT):
            o = result(act, (("in", "kv"), t))
            nc.scalar.activation(GV[:, t, :], o[:, 128:256], Copy)
            drain(nc.scalar.activation(QK5[:, t, 512:640], o[:, 0:128], Copy), (("in", "kv"), t))
        for nme, v, after in (("su", SU, "sv"), ("sv", SV, "ga0")):
            split_next(("in", after))
            for t in range(NT):
                move((("in", nme), t), v[:, t, :], func=ACT.Gelu_apprx_tanh)
        for nme, v, h, after in (("ga0", GA, 0, "ga1"), ("ga1", GA, 1, "gb0"), ("gb0", GBT, 0, "gb1"), ("gb1", GBT, 1, None)):
            if after:
                split_next(("in", after))
            for t in range(NT):
                move((("in", nme), t), v[:, t, 512 * h:512 * h + 512], func=ACT.Sigmoid)
        turn_out("gq", 4, lambda c: GQT[:, c, :])
        turn_out("gk", 2, lambda c: GKT[:, c, :])

        def ada_copy(n):
            move(("ada", n), AROW[:, 0, :])

        def attention(tag, heads, scale, fillers):
            def exps(h):
                act.wait_ge(S(f"{tag}_max"), h + 1)
                if h >= 2:
                    result(act, (tag, "p", h - 2))
                o = result(act, (tag, "s", h))
                for t in range(NT):
                    ins = nc.scalar.activation(prob_buf[tag][h % 2][:, t, :], o[:, t * SEQ:(t + 1) * SEQ], ACT.Exp,
                                               bias=SX[:, h % 2, 0, t:t + 1], scale=scale, accum_out=SX[:, h % 2, 1, t:t + 1])
                drain(ins, (tag, "s", h))

            exps(0)
            for h in range(heads):
                if h + 1 < heads:
                    exps(h + 1)
                if h < len(fillers):
                    ada_copy(fillers[h])
                if h >= 2:
                    result(act, (tag, "v", h - 2))
                move((tag, "p", h), probT_buf[tag][h % 2])

        attention("g", 8, ATT_SCALE, list(range(8)))
        split_next(("att_out", 0))
        turn_split("sg", 4, 4)
        split_next(("sgu_out", 0))
        split_next(("w_out", 0))
        turn_split("mg", KC)
        split_next(("w_out", 1))
        split_next(("cq", 0))
        turn_split("xc", KC)
        for f in range(2):
            move((("cq", 0), f), halves(CQT[:, 2 * f:2 * f + 2, :]))
        attention("c", 4, X_SCALE, list(range(8, 12)))
        split_next(("co", 0))

        def gate_out(s):
            for h in range(2):
                move(("gate", s, h), GB[:, h * 512:(h + 1) * 512])

        def moe(L):
            if L > 0:
                act.wait_ge(S("ada_set"), 2 * L)
            turn_out(("moe", L), KC, lambda c: hT[:, c, :])
            load_table(ACT.Exp)
            if L == 0:
                act.wait_ge(m(L, "rt0"), 1)
                nc.scalar.activation(RT[:, 128:136], RT[:, 128:136], ACT.Exp).then_inc(m(L, "re0"), 1)
            else:
                act.wait_ge(m(L, "rt0"), 1)
                nc.scalar.activation(RT[:, 128:160], RT[:, 128:160], ACT.Exp).then_inc(m(L, "re0"), 1)
            act.wait_ge(m(L, "rt1"), 1)
            nc.scalar.activation(RT[:, 224:226], RT[:, 224:226], ACT.Exp).then_inc(m(L, "re1"), 1)
            if L > 0:
                gate_out(2 * L - 1)
            load_table(ACT.Silu)

            def swt_out(a, done):
                nc.scalar.activation(SELT_[a], ps[:, B_TR, 0:SEQ], Copy)
                nc.scalar.activation(WSLOT[a], ps[:, B_TR, SEQ:SEQ + 1], Copy).then_inc(done, 1)

            def silu(a, done):
                nc.scalar.activation(SG[a][CAP:P, :], ps[0:CAP, B_GU, :], ACT.Silu).then_inc(done, 1)

            def ht_out(a, done):
                nc.scalar.activation(HT[a].rearrange("p c s -> p (c s)"), ps[:, B_GU, 0:SEQ], Copy).then_inc(done, 1)

            def yh_out(a, done):
                nc.scalar.activation(YH[a], ps[:, B_Y, :], Copy, scale=WSLOT[a]).then_inc(done, 1)

            def expert(e, a, final):
                wait_expert(act, L, "gu", e + 1)
                wait_expert(act, L, "h", e - 1)
                silu(a, S("expert_sg"))
                wait_expert(act, L, "htp", e + 1)
                wait_expert(act, L, "y", e - 1)
                ht_out(a, S("expert_ht"))
                if not final:
                    wait_expert(act, L, "xg", e + 2)
                    wait_expert(act, L, "scat", e)
                    swt_out(1 - a, S("expert_swt"))
                wait_expert(act, L, "y", e + 1)
                wait_expert(act, L, "scat", e - 1)
                wait_expert(act, L, "swt", e + 1)
                yh_out(a, S("expert_yh"))
                nb = act.value_load(TBL[0:1, L, 0, bass.ds(e, 1)], min_val=0, max_val=3)
                b1 = act.value_load(TBL[0:1, L, 1, bass.ds(e, 1)], min_val=1, max_val=48)
                with act.If(nb > 0):
                    with act.Fori(0, nb) as j:
                        act.wait_ge(m(L, "x_xg"), b1 + j)
                        act.wait_ge(m(L, "xdone"), b1 + j)
                        swt_out(2, m(L, "x_swt"))
                        act.wait_ge(m(L, "x_gu"), b1 + j + 1)
                        silu(2, m(L, "x_sg"))
                        act.wait_ge(m(L, "x_htp"), b1 + j)
                        ht_out(2, m(L, "x_ht"))
                        act.wait_ge(m(L, "x_y"), b1 + j)
                        act.wait_ge(m(L, "x_swt"), b1 + j)
                        yh_out(2, m(L, "x_yh"))

            wait_expert(act, L, "xg", 1)
            swt_out(0, S("expert_swt"))
            act.wait_ge(m(L, "table"), 1)
            expert(0, 0, False)
            expert(1, 1, False)
            with act.Fori(1, NE // 2 - 1) as i:
                for a in range(2):
                    expert(2 * i + a, a, False)
            expert(NE - 2, 0, False)
            expert(NE - 1, 1, True)

        if NLAYER > 0:
            moe(0)
        if ("sb", 0) in order:
            act.wait_ge(S("ada_set"), 1)
            result(act, ("y", 0, 3))
            split_next(("sb", 0))
            turn_split("sbx", KC)
            for j in range(4):
                split_next(("sb", j + 1))
                for f in range(2):
                    q = 4 * (j % 2) + 2 * f
                    move((("sb", j), f), halves((SQT if j < 2 else SKT)[:, q:q + 2, :]), scale=(ATT_SCALE if j < 2 else 1.0))
            for j in range(4, 6):
                if j == 4:
                    split_next(("sb", 5))
                for t in range(NT):
                    move((("sb", j), t), SBV[:, t, 512 * (j - 4):512 * (j - 3)])
            gate_out(0)
            for h in range(16):
                move(("z1", h), SE[:, h, :], slice(0, 384), ACT.Abs)
                if h % 4 == 3:
                    read(act, ("z1", h))
                    g = SE[:, h - 3:h + 1, :]
                    nc.scalar.activation(g, g, ACT.Exp, scale=-1.0).then_inc(S("exp_abs"), 1)
            for q in range(4):
                act.wait_ge(S("exp_abs"), q + 1)
                g = SE[:, 4 * q:4 * q + 4, :]
                nc.scalar.activation(g, g, ACT.Ln, bias=1.0).then_inc(S("log1p"), 1)
            for h in range(16):
                act.wait_ge(S("logit"), h + 1)
                move(("z2", h), SE[:, h, :], slice(0, 384), ACT.Exp)
            split_next(("sb_out", 0))
            split_next(("sb_out", 1))
        if NLAYER > 1:
            moe(1)
        if ("ret", 0) in order:
            act.wait_ge(S("ada_set"), 3)
            result(act, ("y", 1, 3))
            split_next(("ret", 0))
            turn_split("rx", KC)
            for j in range(4):
                split_next(("ret", j + 1))
                for t in range(NT):
                    move((("ret", j), t), (RQRAW if j < 2 else RKRAW)[:, t, 512 * (j % 2):512 * (j % 2) + 512])
            act.wait_ge(S("ret_roped"), 1)
            for j in range(4, 6):
                split_next(("ret", j + 1))
                for t in range(NT):
                    move((("ret", j), t), RV[:, t, 512 * (j - 4):512 * (j - 3)])
            turn_out("rq", KC, lambda c: RQT[:, c, :])
            turn_out("rk", KC, lambda c: RKT[:, c, :])
            for j in range(6, 8):
                split_next(("ret", j + 1))
                for t in range(NT):
                    move((("ret", j), t), RV[:, t, 512 * (j - 4):512 * (j - 3)])
            for j in range(8, 12):
                if j < 11:
                    split_next(("ret", j + 1))
                for t in range(NT):
                    move((("ret", j), t), RG[:, t, 512 * (j - 8):512 * (j - 7)], func=ACT.Silu)
            gate_out(2)
            split_next(("ret_out", 0))
            turn_split("ro", 16)
            for j in range(1, 4):
                split_next(("ret_out", j))
        if NLAYER > 2:
            moe(2)

    norms = []
    @block.vector
    def _(dve):
        V = nc.vector
        chain = [0]

        def link(ins):
            chain[0] += 1
            ins.then_inc(S("dve"), 1)
            dve.wait_ge(S("dve"), chain[0])

        def power(n, par):
            norms.append((n, par))

        def rstd(k):
            dve.wait_ge(S("rstd"), k)

        def moments(x, width, eps, rms, par=0):
            k = max(1, width // 512)
            for t in range(NT):
                for i in range(k):
                    w = width // k
                    ins = V.bn_stats(ST[:, par, t, i, :], x(t)[:, i * w:(i + 1) * w])
            link(ins)
            for t in range(NT):
                ins = V.bn_aggr(MV[:, par, t, :], ST[:, par, t, 0:k, :])
            link(ins)
            mean, var = MV[:, par, :, 0], MV[:, par, :, 1]
            if rms:
                link(V.tensor_tensor(MS[:, par, 0:NT], mean, mean, ALU.mult))
                ins = V.scalar_tensor_tensor(out=MS[:, par, 0:NT], in0=MS[:, par, 0:NT], scalar=eps, in1=var, op0=ALU.add, op1=ALU.add)
            else:
                ins = V.tensor_scalar(MS[:, par, 0:NT], var, eps, None, ALU.add)
            ins.then_inc(S("square"), 1)
            power(NT, par)
            return len(norms)

        def rms_to(dst, x, done):
            rstd(moments(lambda t: x[:, t, :], D, EPS_RMS, True))
            for t in range(NT):
                ins = V.tensor_scalar(dst[:, t, :], x[:, t, :], RS[:, 0, t:t + 1], None, ALU.mult)
            ins.then_inc(done, 1)

        def turn_out(key, chunks, dest):
            scale, shift = TURN.get(key, (None, None))
            for j in range(1, (chunks + 1) // 2, 2):
                o = result(dve, (key, j))
                for c in (2 * j, 2 * j + 1):
                    i = o[:, (c % 2) * SEQ:(c % 2) * SEQ + SEQ]
                    if shift:
                        ins = V.tensor_scalar(dest(c), i, scale(c), shift(c), ALU.mult, ALU.add)
                    elif scale:
                        ins = V.tensor_scalar(dest(c), i, scale(c), None, ALU.mult)
                    else:
                        ins = V.tensor_copy(dest(c), i)
                drain(ins, (key, j))

        turned_banks = [0]

        def turn_split(key, chunks, at=0):
            scale, shift = TURN.get(key, (None, None))
            for j in range((chunks + 1) // 2):
                turned_banks[0] += 1
                dve.wait_ge(S("turned_hi"), turned_banks[0])
                o = result(dve, (key, j))
                if shift:
                    for c in (2 * j, 2 * j + 1):
                        ins = V.tensor_scalar(hT[:, c, :], o[:, (c % 2) * SEQ:(c % 2) * SEQ + SEQ], scale(c), shift(c), ALU.mult, ALU.add)
                    link(ins)
                    both = slice(2 * j, 2 * j + 2)
                    drain(V.tensor_tensor(HTL[:, both, :], hT[:, both, :], HTH[:, both, :].bitcast(F32), ALU.subtract), (key, j))
                    continue
                for c in (2 * j, 2 * j + 1):
                    i = o[:, (c % 2) * SEQ:(c % 2) * SEQ + SEQ]
                    hi, lo = high(at + c).bitcast(F32), low(at + c)
                    if scale:
                        ins = V.scalar_tensor_tensor(out=lo, in0=i, scalar=scale(c), in1=hi, op0=ALU.mult, op1=ALU.subtract)
                    else:
                        ins = V.tensor_tensor(lo, i, hi, ALU.subtract)
                drain(ins, (key, j))

        def split_values(key, rows, c):
            o = result(dve, key)
            link(V.tensor_copy(HTH[rows, c, :], o[rows, 0:SEQ]))
            drain(V.tensor_tensor(HTL[rows, c, :], o[rows, 0:SEQ], HTH[rows, c, :].bitcast(F32), ALU.subtract), key)

        dve.wait_ge(S("mem_in"), 16)
        rms_to(MEMN, MEM, S("xn_ready"))
        for i, r in enumerate((60, 96)):
            o = result(dve, ("vec", i))
            drain(V.tensor_copy(VT[:, i, 0:r], o[:, 0:r]), ("vec", i))
        read(dve, ("vec", 0))
        turn_split("mem", KC)
        dve.wait_ge(S("x_in"), 16)
        rms_to(XN, X, S("xn_ready"))
        turn_split("x", KC)
        o = result(dve, ("ws", 0))
        drain(V.tensor_copy(WST[:, :, :].rearrange("p g q -> p (g q)"), o), ("ws", 0))
        dve.wait_ge(S("pos_in"), 16)
        dve.wait_ge(S("cst_in"), 16)
        link(V.tensor_copy(POSF[:, :], POS[:, :]))
        link(V.tensor_tensor(ANG.rearrange("p (t i) -> p t i", t=NT), bc(POSF[:, :], [NT, 64], 2), bc(cst(C_INVF, 64), [NT, 64], 1), ALU.mult))
        V.tensor_scalar(KK[:, 0, :], ANG, 1.0 / (2 * np.pi), 0.25, ALU.mult, ALU.add)
        link(V.tensor_scalar(KK[:, 1, :], ANG, 1.0 / (2 * np.pi), None, ALU.mult))
        magic = 1.5 * 2.0 ** 23
        link(V.tensor_scalar(KK, KK, magic, None, ALU.add))
        link(V.tensor_scalar(KK, KK, magic, None, ALU.subtract))
        link(V.scalar_tensor_tensor(out=RR, in0=KK, scalar=-6.28125, in1=bc(ANG, [2, 128], 1), op0=ALU.mult, op1=ALU.add))
        link(V.scalar_tensor_tensor(out=RR, in0=KK, scalar=-(2 * np.pi - 6.28125), in1=RR, op0=ALU.mult, op1=ALU.add))
        link(V.tensor_scalar(RR[:, 0, :], RR[:, 0, :], np.pi / 2, None, ALU.add))
        V.tensor_scalar(RR, RR, 3.1415925, -3.1415925, ALU.min, ALU.max).then_inc(S("angles"), 1)

        def ada_sum(n):
            o = result(dve, ("adac", n))
            drain(V.tensor_tensor(ADA[:, 4 * n:4 * n + 4], o[:, 0:4], VT[:, 1, 4 * n:4 * n + 4], ALU.add), ("adac", n))
            if n % 6 == 5:
                read(dve, ("adac", n))
                v = ADA[:, 4 * n - 12:4 * n + 4]
                V.tensor_scalar(v, v, 1.0, None, ALU.add).then_inc(S("ada_set"), 1)

        def ada_dot(n):
            r, landed_at, _ = place[("ada", n), 0]
            dve.wait_ge(landed[r], landed_at)
            if n >= ADA_PE + 2:
                result(dve, ("adac", n - 2))
            w = slot(r).rearrange("p (c n) -> p c n", n=512)
            acc = AROW[:, n % 2, :]
            ins = V.tensor_scalar(acc, w[:, 0, :], SILC[:, 0, 0:1], None, ALU.mult)
            for c in range(1, KC):
                link(ins)
                ins = V.scalar_tensor_tensor(out=acc, in0=w[:, c, :], scalar=SILC[:, c, 0:1], in1=acc, op0=ALU.mult, op1=ALU.add)
            ins.then_inc(S("ada_acc"), 1)

        dve.wait_ge(S("small_in"), 16 * 10)
        for t in range(NT):
            read(dve, (("in", "q"), t))
            read(dve, (("in", "kv"), t))
        qk4 = QK5.rearrange("p t (h d) -> p t h d", d=64)
        link(V.tensor_tensor(R5, QK5, QK5, ALU.mult))
        link(V.tensor_reduce(MS[:, 1, 0:20].rearrange("p (t h) -> p t h", t=NT), R5.rearrange("p t (h d) -> p t h d", d=64), AX, ALU.add))
        V.tensor_scalar(MS[:, 1, 0:20], MS[:, 1, 0:20], 1.0 / 64, EPS_RMS, ALU.mult, ALU.add).then_inc(S("square"), 1)
        power(20, 1)
        rstd(len(norms))
        for t in range(NT):
            ins = V.tensor_tensor(qk4[:, t], qk4[:, t], bc(RS[:, 1, 10 * t:10 * t + 10], [10, 64], 2), ALU.mult)
        link(ins)
        link(V.tensor_tensor(QK5, QK5, bc(GQK[:, :, :].rearrange("p h d -> p (h d)"), [NT, 640], 1), ALU.mult))
        pairs = QK5.rearrange("p t (h i two) -> p t h i two", two=2, i=32)
        rot = R5.rearrange("p t (h i two) -> p t h i two", two=2, i=32)
        for t in range(NT):
            cos = bc(cst(C_ROPE + 64 * t, 32), [10, 32], 1)
            sin = bc(cst(C_ROPE + 64 * t + 32, 32), [10, 32], 1)
            x0, x1 = pairs[:, t, :, :, 0], pairs[:, t, :, :, 1]
            t1 = TMP[:, 0, 0:320].rearrange("p (h i) -> p h i", i=32)
            t2 = TMP[:, 1, 0:320].rearrange("p (h i) -> p h i", i=32)
            for o, c1, c2, op in ((rot[:, t, :, :, 0], cos, sin, ALU.subtract), (rot[:, t, :, :, 1], sin, cos, ALU.add)):
                V.tensor_tensor(t1, x0, c1, ALU.mult)
                link(V.tensor_tensor(t2, x1, c2, ALU.mult))
                link(V.tensor_tensor(o, t1, t2, op))
        for t in range(NT):
            for r in range(2):
                kd = KD[:, t, :].rearrange("p (v r d) -> p v r d", v=2, r=2)
                ins = V.tensor_copy(kd[:, :, r, :], R5[:, t, 512:640].rearrange("p (v d) -> p v d", v=2))
        ins.then_inc(S("qk_roped"), 1)
        for t in range(NT):
            read(dve, (("in", "sv"), t))
        rstd(moments(lambda t: SV[:, t, :], 512, EPS_RMS, False))
        for t in range(NT):
            link(V.tensor_scalar(SV[:, t, :], SV[:, t, :], MV[:, 0, t, 0:1], RS[:, 0, t:t + 1], ALU.subtract, ALU.mult))
            link(V.tensor_tensor(SV[:, t, :], SV[:, t, :], SGB[:, 0, :], ALU.mult))
            V.tensor_tensor(SV[:, t, :], SV[:, t, :], SGB[:, 1, :], ALU.add).then_inc(S("sv_normed"), 1)
        turn_out("gq", 4, lambda c: GQT[:, c, :])


        def attention(tag, heads, scale, fillers, out_rows):
            def maxima(h):
                o = result(dve, (tag, "s", h))
                link(V.tensor_reduce(SX[:, h % 2, 0, :], o.rearrange("p (t k) -> p t k", t=NT), AX, ALU.max))
                V.tensor_scalar(SX[:, h % 2, 0, :], SX[:, h % 2, 0, :], -scale, None, ALU.mult).then_inc(S(f"{tag}_max"), 1)

            def normalise(h):
                read(dve, (tag, "s", h))
                link(V.reciprocal(SX[:, h % 2, 2, :], SX[:, h % 2, 1, :]))
                for t in range(NT):
                    pr = prob_buf[tag][h % 2][:, t, :]
                    ins = V.tensor_scalar(pr, pr, SX[:, h % 2, 2, t:t + 1], None, ALU.mult)
                ins.then_inc(S(f"{tag}_probs"), 1)

            def values_out(h):
                split_values((tag, "v", h), *out_rows(h))

            maxima(0)
            for h in range(heads):
                if h + 1 < heads:
                    maxima(h + 1)
                normalise(h)
                if 1 <= h <= len(fillers):
                    ada_sum(fillers[h - 1])
                if h >= 1:
                    values_out(h - 1)
            values_out(heads - 1)
            if len(fillers) >= heads:
                ada_sum(fillers[heads - 1])

        def half_rows(h):
            return slice(64 * (h % 2), 64 * (h % 2) + 64)
        attention("g", 8, ATT_SCALE, list(range(8)), lambda h: (half_rows(h), h // 2))
        for t in range(NT):
            read(dve, (("in", "su"), t))
            o = result(dve, ("sgu", t))
            for g in range(4):
                v = SU[:, t, g * P:(g + 1) * P]
                ins = V.scalar_tensor_tensor(out=v, in0=o[:, g * P:(g + 1) * P], scalar=VT[:, 0, V_BS + g:V_BS + g + 1], in1=v, op0=ALU.add, op1=ALU.mult)
            drain(ins, ("sgu", t))
        turn_split("sg", 4, 4)
        for t in range(NT):
            for h in range(2):
                read(dve, (("in", f"ga{h}"), t))
                v = GA[:, t, 512 * h:512 * h + 512]
                drain(V.tensor_tensor(v, result(dve, ("att_out", "o", t, h)), v, ALU.mult), ("att_out", "o", t, h))
        for t in range(NT):
            for h in range(2):
                read(dve, (("in", f"gb{h}"), t))
                v, g = GBT[:, t, 512 * h:512 * h + 512], GA[:, t, 512 * h:512 * h + 512]
                drain(V.tensor_tensor(v, result(dve, ("sgu_out", "o", t, h)), v, ALU.mult), ("sgu_out", "o", t, h))
                read(dve, ("sgu_out", "o", t, h))
                read(dve, ("att_out", "o", t, h))
                V.tensor_tensor(g, g, v, ALU.add).then_inc(S("merged"), 1)
        turn_split("mg", KC)

        def residual(keys):
            for t in range(NT):
                for h in range(2):
                    v = X[:, t, 512 * h:512 * h + 512]
                    drain(V.tensor_tensor(v, result(dve, keys(t, h)), v, ALU.add), keys(t, h))
            for t in range(NT):
                for h in range(2):
                    read(dve, keys(t, h))

        residual(lambda t, h: ("w_out", "o", t, h))
        rms_to(XN, X, S("xn_ready"))
        turn_split("xc", KC)
        attention("c", 4, X_SCALE, list(range(8, 12)), lambda h: (slice(0, P), h))
        residual(lambda t, h: ("co", "o", t, h))

        def top_two(L, logits, gidx):
            oh = RT[:, 160:192].rearrange("p (t e) -> p t e", t=NT)
            em = RT[:, 192:224].rearrange("p (t e) -> p t e", t=NT)
            link(V.tensor_tensor(oh, bc(cst(C_GRP, 16), [NT, 16], 1), gidx.broadcast_to([P, NT, 16]), ALU.is_equal))
            link(V.tensor_tensor(em, logits, oh, ALU.mult))
            link(V.tensor_scalar(oh, oh, BIG, -BIG, ALU.mult, ALU.add))
            link(V.tensor_tensor(em, em, oh, ALU.add))
            v8 = RT[:, 232:248].rearrange("p (t e) -> p t e", t=NT)
            link([V.max(v8[:, t, :], em[:, t, :]) for t in range(NT)][-1])
            link([V.max_index(RTI[:, 1, t, :], v8[:, t, :], em[:, t, :]) for t in range(NT)][-1])
            V.tensor_tensor(RT[:, 224:226], v8[:, :, 1], v8[:, :, 0], ALU.subtract).then_inc(m(L, "rt1"), 1)

        def diag(s):
            dve.wait_ge(S("ada_set"), s + 1)
            V.tensor_tensor(GB[:, :].rearrange("p (c n) -> p c n", n=P), bc(ident, [KC, P], 1),
                            ADA[:, 24 * s + 16:24 * s + 24].unsqueeze(2).broadcast_to([P, KC, P]), ALU.mult).then_inc(S("diag"), 1)

        def moe(L):
            if L == 0:
                rms_to(XN, X, S("xn_ready"))
            V.memset(YH[0].bitcast(F32), 0.0).then_inc(m(L, "zero"), 1)
            pad = RT[:, 304:320].rearrange("p (t e) -> p t e", t=NT)
            V.memset(pad, -BIG)
            turn_out(("moe", L), KC, lambda c: hT[:, c, :])
            if L > 0:
                diag(2 * L - 1)
            nr = 20 if L == 0 else 16
            o = result(dve, ("route", L))[:, 0:64].rearrange("p (t e) -> p t e", t=NT)[:, :, 0:nr]
            lg = RT[:, 256:256 + 2 * nr].rearrange("p (t e) -> p t e", t=NT)
            drain(V.tensor_tensor(lg, o, bc((BR1 if L == 0 else BR2)[:, :], [NT, nr], 1), ALU.add), ("route", L))
            read(dve, ("route", L))
            g8 = RT[:, 320:336].rearrange("p (t e) -> p t e", t=NT)
            gsum, gval = RT[:, 336:338], RT[:, 338:340]
            if L == 0:
                el = lg[:, :, 4:20]
                link(V.tensor_copy(pad[:, :, 0:4], lg[:, :, 0:4]))
            else:
                el = lg
                l8 = RT[:, 340:356].rearrange("p (t e) -> p t e", t=NT)
                link([V.max(l8[:, t, :], lg[:, t, :]) for t in range(NT)][-1])
                pr = RT[:, 128:160].rearrange("p (t e) -> p t e", t=NT)
                V.tensor_tensor(pr, lg, l8[:, :, 0:1].broadcast_to([P, NT, 16]), ALU.subtract).then_inc(m(L, "rt0"), 1)
                dve.wait_ge(m(L, "re0"), 1)
                link(V.tensor_reduce(gsum, pr, AX, ALU.add))
                link(V.reciprocal(gval, gsum))
                link(V.tensor_tensor(pr, pr, gval.unsqueeze(2).broadcast_to([P, NT, 16]), ALU.mult))
                q = RT[:, 128:160].rearrange("p (g k) -> p g k", k=4)
                pairs_ = RT[:, 360:408].rearrange("p (g k) -> p g k", k=6)
                V.tensor_tensor(pairs_[:, :, 0:3], q[:, :, 0:3], q[:, :, 1:4], ALU.add)
                V.tensor_tensor(pairs_[:, :, 3:5], q[:, :, 0:2], q[:, :, 2:4], ALU.add)
                link(V.tensor_tensor(pairs_[:, :, 5:6], q[:, :, 0:1], q[:, :, 3:4], ALU.add))
                gs = RT[:, 408:416]
                link(V.tensor_reduce(gs, pairs_, AX, ALU.max))
                link(V.tensor_copy(pad[:, :, 0:4], gs.rearrange("p (t g) -> p t g", t=NT)))
            link([V.max(g8[:, t, :], pad[:, t, :]) for t in range(NT)][-1])
            link([V.max_index(RTI[:, 0, t, :], g8[:, t, :], pad[:, t, :]) for t in range(NT)][-1])
            gidx = RT[:, 356:358]
            link(V.tensor_copy(gidx, RTI[:, 0, :, 0]))
            if L == 0:
                ex = RT[:, 128:136].rearrange("p (t e) -> p t e", t=NT)
                V.tensor_tensor(ex, lg[:, :, 0:4], g8[:, :, 0:1].broadcast_to([P, NT, 4]), ALU.subtract).then_inc(m(L, "rt0"), 1)
                dve.wait_ge(m(L, "re0"), 1)
                link(V.tensor_reduce(gsum, ex, AX, ALU.add))
                link(V.reciprocal(gval, gsum))
            top_two(L, el, gidx.unsqueeze(2))
            i2 = RT[:, 420:424].rearrange("p (t k) -> p t k", t=NT)
            link(V.tensor_copy(i2, RTI[:, 1, :, 0:2]))
            o1 = RT[:, 424:456].rearrange("p (t e) -> p t e", t=NT)
            o2 = RT[:, 456:488].rearrange("p (t e) -> p t e", t=NT)
            V.tensor_tensor(o1, bc(cst(C_EXP, 16), [NT, 16], 1), i2[:, :, 0:1].broadcast_to([P, NT, 16]), ALU.is_equal)
            link(V.tensor_tensor(o2, bc(cst(C_EXP, 16), [NT, 16], 1), i2[:, :, 1:2].broadcast_to([P, NT, 16]), ALU.is_equal))
            V.tensor_tensor(SELT, o1, o2, ALU.add).then_inc(m(L, "chosen"), 1)
            dve.wait_ge(m(L, "re1"), 1)
            w1, w2 = RT[:, 226:228], RT[:, 228:230]
            link(V.tensor_scalar(w1, RT[:, 224:226], 1.0, None, ALU.add))
            link(V.reciprocal(w1, w1))
            if L == 0:
                link(V.tensor_tensor(w1, w1, gval, ALU.mult))
            link(V.tensor_tensor(w2, w1, RT[:, 224:226], ALU.mult))
            V.tensor_tensor(o1, o1, w1.unsqueeze(2).broadcast_to([P, NT, 16]), ALU.mult)
            link(V.tensor_tensor(o2, o2, w2.unsqueeze(2).broadcast_to([P, NT, 16]), ALU.mult))
            link(V.tensor_tensor(COMB, o1, o2, ALU.add))
            dve.wait_ge(m(L, "chosen"), 1)
            o = result(dve, ("rank", L))
            V.tensor_copy(TBF[0:1, 0, :], o[0:1, 32:48])
            link(V.scalar_tensor_tensor(out=RANK, in0=o[:, 0:32].rearrange("p (t e) -> p t e", t=NT), scalar=1.0, in1=SELT, op0=ALU.add, op1=ALU.mult))
            drain(V.tensor_scalar(RANK, RANK, -1.0, None, ALU.add), ("rank", L))
            read(dve, ("rank", L))
            slots = cst(C_SLOT)
            if L == 0:
                gain, shift = VT[:, 0, V_MOE:V_MOE + 8], None
            else:
                s = 24 * (2 * L - 1)
                gain, shift = ADA[:, s + 8:s + 16], ADA[:, s:s + 8]

            def choose(a, rank, e, done):
                V.tensor_copy(WTOK[a].unsqueeze(2), COMB[:, :, bass.ds(e, 1)])
                for t in range(NT):
                    ins = V.tensor_scalar(SEL_[a][:, t, :], slots, rank(t), None, ALU.is_equal)
                ins.then_inc(done, 1)

            def ranks(e):
                return lambda t: RANK[:, t, bass.ds(e, 1)]

            def xe_out(a, done, mid, at):
                xg = ps[:, B_XG, :].rearrange("p (c s) -> p c s", s=CAP)
                gs_ = gain.unsqueeze(2).broadcast_to([P, KC, CAP])
                if shift is None:
                    V.tensor_tensor(XE[a], xg, gs_, ALU.mult).then_inc(done, 1)
                    return
                V.tensor_tensor(XE[a], xg, gs_, ALU.mult).then_inc(mid, 1)
                dve.wait_ge(mid, at)
                V.tensor_tensor(XE[a], XE[a], shift.unsqueeze(2).broadcast_to([P, KC, CAP]), ALU.add).then_inc(done, 1)

            def hidden(a, done):
                V.tensor_tensor(HH[a][CAP:P, :], ps[CAP:P, B_GU, :], SG[a][CAP:P, :], ALU.mult).then_inc(done, 1)

            def yl_out(a, done):
                V.scalar_tensor_tensor(out=YL[a], in0=ps[:, B_Y, :], scalar=WSLOT[a], in1=YH[a].bitcast(F32),
                                       op0=ALU.mult, op1=ALU.subtract).then_inc(done, 1)

            def expert(e, a, build_next, final):
                wait_expert(dve, L, "sg", e + 1)
                wait_expert(dve, L, "htp", e - 1)
                hidden(a, S("expert_h"))
                if build_next:
                    wait_expert(dve, L, "xg", e + 1)
                    choose(a, ranks(e + 2), e + 2, S("expert_sel"))
                if not final:
                    wait_expert(dve, L, "xg", e + 2)
                    wait_expert(dve, L, "gu", e)
                    xe_out(1 - a, S("expert_xe"), S("expert_xm"), NE * (L - 1) + e + 2)
                wait_expert(dve, L, "yh", e + 1)
                wait_expert(dve, L, "scat", e - 1)
                yl_out(a, S("expert_ye"))
                nb = dve.value_load(TBL[0:1, L, 0, bass.ds(e, 1)], min_val=0, max_val=3)
                b1 = dve.value_load(TBL[0:1, L, 1, bass.ds(e, 1)], min_val=1, max_val=48)
                with dve.If(nb > 0):
                    with dve.Fori(0, nb) as j:
                        V.tensor_tensor(RKX.unsqueeze(2), RANK[:, :, bass.ds(e, 1)], CST[:, bass.ds(C_OFF + j, 1)].unsqueeze(1).broadcast_to([P, NT, 1]), ALU.subtract).then_inc(m(L, "x_rk"), 1)
                        dve.wait_ge(m(L, "x_rk"), b1 + j)
                        choose(2, lambda t: RKX[:, t:t + 1], e, m(L, "x_sel"))
                        dve.wait_ge(m(L, "x_xg"), b1 + j)
                        xe_out(2, m(L, "x_xe"), m(L, "x_xm"), b1 + j)
                        dve.wait_ge(m(L, "x_sg"), b1 + j)
                        hidden(2, m(L, "x_h"))
                        dve.wait_ge(m(L, "x_yh"), b1 + j)
                        dve.wait_ge(m(L, "xdone"), b1 + j)
                        yl_out(2, m(L, "x_ye"))

            dve.wait_ge(m(L, "xdone"), 1)
            choose(0, ranks(0), 0, S("expert_sel"))
            for b in range(1, 4):
                ins = V.tensor_scalar(TBF[0:1, b, :], TBF[0:1, 0, :], b * CAP + 0.5, None, ALU.is_gt)
            link(ins)
            link(V.tensor_tensor(TBF[0:1, 4, :], TBF[0:1, 1, :], TBF[0:1, 2, :], ALU.add))
            link(V.tensor_tensor(TBF[0:1, 4, :], TBF[0:1, 4, :], TBF[0:1, 3, :], ALU.add))
            link(V.memset(TBF[0:1, 6, :], 1.0))
            link(V.tensor_tensor_scan(TBF[0:1, 5, :], TBF[0:1, 6, :], TBF[0:1, 4, :], 1.0, ALU.mult, ALU.add))
            link(V.tensor_tensor(TBF[0:1, 7, :], TBF[0:1, 5, :], TBF[0:1, 4, :], ALU.subtract))
            V.tensor_copy(TBL[0:1, L, 0, :], TBF[0:1, 4, :])
            V.tensor_copy(TBL[0:1, L, 1, :], TBF[0:1, 7, :])
            V.tensor_copy(TBL[0:1, L, 2, :], TBF[0:1, 5, :]).then_inc(m(L, "table"), 1)
            choose(1, ranks(1), 1, S("expert_sel"))
            dve.wait_ge(m(L, "table"), 1)
            wait_expert(dve, L, "xg", 1)
            xe_out(0, S("expert_xe"), S("expert_xm"), NE * (L - 1) + 1)
            expert(0, 0, True, False)
            expert(1, 1, True, False)
            with dve.Fori(1, NE // 2 - 1) as i:
                for a in range(2):
                    expert(2 * i + a, a, True, False)
            expert(NE - 2, 0, False, False)
            expert(NE - 1, 1, False, True)

        def deepnorm(keys, s, k):
            for h in range(2):
                read(dve, ("gate", s, h))
            for t in range(NT):
                for h in range(2):
                    o = result(dve, keys(t, h))
                    tmp = SM[:, :, :].rearrange("p a b -> p (a b)")[:, 0:512]
                    drain(V.tensor_tensor(tmp, o, GB[:, 512 * h:512 * h + 512], ALU.mult), keys(t, h))
                    read(dve, keys(t, h))
                    v = X[:, t, 512 * h:512 * h + 512]
                    link(V.scalar_tensor_tensor(out=v, in0=v, scalar=ALPHA, in1=tmp, op0=ALU.mult, op1=ALU.add))
            rstd(moments(lambda t: X[:, t, :], D, EPS_LN, False))
            dve.wait_ge(S("gains_in"), 16 + 32 * k)
            for t in range(NT):
                v = X[:, t, :]
                link(V.tensor_scalar(v, v, MV[:, 0, t, 0:1], RS[:, 0, t:t + 1], ALU.subtract, ALU.mult))
                link(V.tensor_tensor(v, v, LNG[:, 0, :], ALU.mult))
                ins = V.tensor_tensor(v, v, LNG[:, 1, :], ALU.add)
                if t == 0:
                    link(ins)
            ins.then_inc(S("x_ready"), 1)
            dve.wait_ge(S("x_ready"), k + 1)

        if NLAYER > 0:
            moe(0)
            residual(lambda t, h: ("y", 0, 2 * t + h))
            rstd(moments(lambda t: X[:, t, :], D, EPS_RMS, True))
            dve.wait_ge(S("gains_in"), 16)
            for t in range(NT):
                v = X[:, t, :]
                ins = V.scalar_tensor_tensor(out=v, in0=v, scalar=RS[:, 0, t:t + 1], in1=LNG[:, 0, :], op0=ALU.mult, op1=ALU.mult)
            ins.then_inc(S("x_ready"), 1)
            dve.wait_ge(S("x_ready"), 1)
        if ("sb", 0) in order:
            diag(0)
            turn_split("sbx", KC)

            def weights(h):
                dve.wait_ge(S("log1p"), 4)
                o = result(dve, ("z2", h))
                e = SE[:, h, :]
                link(V.scalar_tensor_tensor(out=e, in0=o[:, 0:384], scalar=0.0, in1=e, op0=ALU.max, op1=ALU.add))
                d = e.rearrange("p (b q) -> p b q", b=3)[:, 0:3:2, :]
                V.tensor_tensor(d, d, bc(cst(C_CAUSAL), [2, P], 1), ALU.mult).then_inc(S("sp"), 1)

            def values_out(h):
                split_values(("sv", h), half_rows(h), h // 2)

            dve.wait_ge(S("silu_c"), 1)
            ada_dot(12)
            for n in range(13, 18):
                ada_dot(n)
                ada_sum(n - 1)
            ada_sum(17)
            for h in range(16):
                weights(h)
                if h >= 2:
                    values_out(h - 2)
            values_out(14)
            values_out(15)
            deepnorm(lambda t, h: ("sb_out", "o", t, h), 0, 1)
        if NLAYER > 1:
            moe(1)
            deepnorm(lambda t, h: ("y", 1, 2 * t + h), 1, 2)
        if ("ret", 0) in order:
            turn_split("rx", KC)
            ada_dot(18)
            dve.wait_ge(S("cos_sin"), 1)
            for n, (raw, dst) in enumerate(((RQRAW, RQ), (RKRAW, RK))):
                for j in range(2):
                    for t in range(NT):
                        read(dve, (("ret", 2 * n + j), t))
                x = raw.rearrange("p t (h d) -> p t h d", d=P)
                y = dst.rearrange("p t (h d) -> p t h d", d=P)
                for t in range(NT):
                    cos, sin = (bc(CS2[:, i, t, :], [8, 64], 1) for i in range(2))
                    x1, x2 = x[:, t, :, 0:64], x[:, t, :, 64:128]
                    a1 = RT1[:, t, :].rearrange("p (h i) -> p h i", i=64)
                    a2 = RT2[:, t, :].rearrange("p (h i) -> p h i", i=64)
                    V.tensor_tensor(a1, x1, cos, ALU.mult)
                    link(V.tensor_tensor(a2, x2, sin, ALU.mult))
                    link(V.tensor_tensor(y[:, t, :, 0:64], a1, a2, ALU.subtract))
                    V.tensor_tensor(a1, x2, cos, ALU.mult)
                    link(V.tensor_tensor(a2, x1, sin, ALU.mult))
                    ins = V.tensor_tensor(y[:, t, :, 64:128], a1, a2, ALU.add)
                    if n == 1 and t == 1:
                        ins.then_inc(S("ret_roped"), 1)
                    else:
                        link(ins)
                if n == 0:
                    ada_dot(19)
                    ada_sum(18)
            ada_dot(20)
            ada_sum(19)
            turn_out("rq", KC, lambda c: RQT[:, c, :])
            turn_out("rk", KC, lambda c: RKT[:, c, :])
            for n in range(21, 24):
                ada_dot(n)
                ada_sum(n - 1)
            ada_sum(23)
            diag(2)
            dve.wait_ge(S("decay_in"), 16)

            def decayed(h):
                if h >= 2:
                    result(dve, ("rv", h - 2))
                o = result(dve, ("rs", h))
                drain(V.tensor_tensor(SM[:, h % 2, :], o[:, 0:384], DM[:, 384 * h:384 * h + 384], ALU.mult), ("rs", h))

            def stats(h):
                o = result(dve, ("rv", h))
                return moments(lambda t: o[:, 256 * t:256 * t + 256], 256, EPS_LN, False, h % 2)

            def gated(h, k):
                rstd(k)
                for j in range(8, 12):
                    for t in range(NT):
                        read(dve, (("ret", j), t))
                o = result(dve, ("rv", h))
                for t in range(NT):
                    v = RG[:, t, 256 * h:256 * h + 256]
                    ins = V.scalar_tensor_tensor(out=v, in0=o[:, 256 * t:256 * t + 256], scalar=MV[:, h % 2, t, 0:1], in1=v, op0=ALU.subtract, op1=ALU.mult)
                drain(ins, ("rv", h))
                read(dve, ("rv", h))
                for t in range(NT):
                    v = RG[:, t, 256 * h:256 * h + 256]
                    ins = V.tensor_scalar(v, v, RS[:, h % 2, t:t + 1], None, ALU.mult)
                if h == 7:
                    ins.then_inc(S("ret_gated"), 1)

            decayed(0)
            k_ = {}
            for h in range(8):
                if h < 7:
                    decayed(h + 1)
                k_[h] = stats(h)
                if h >= 1:
                    gated(h - 1, k_[h - 1])
            gated(7, k_[7])
            turn_split("ro", 16)
            deepnorm(lambda t, h: ("ret_out", "o", t, h), 2, 3)
        if NLAYER > 2:
            moe(2)
            deepnorm(lambda t, h: ("y", 2, 2 * t + h), 3, 4)
        if NLAYER == 0:
            V.tensor_copy(POSF[:, 0:1], POSF[:, 0:1]).then_inc(S("x_ready"), 1)

    @block.gpsimd
    def _(pool):
        nc.gpsimd.memset(NEGH[:, :], -0.5).then_inc(S("neg_half"), 1)
        pool.wait_ge(S("neg_half"), 1)
        pool.dma_start(LNG[:, 0, :], A["g_final"].partition_broadcast(P)).then_inc(S("gains_in"), 16)
        done, splits = [0], [0]

        def norm():
            n = done[0]
            if n >= len(norms):
                return
            done[0] += 1
            width, par = norms[n]
            pool.wait_ge(S("square"), n + 1)
            nc.gpsimd.tensor_tensor(RS[:, par, 0:width], MS[:, par, 0:width], NEGH[:, 0:width], ALU.pow).then_inc(S("rstd"), 1)
            if n + 1 in RELOADS:
                i = RELOADS.index(n + 1)
                pool.wait_ge(S("x_ready"), i + 1)
                g, b = A["ln_g_2"][i // 2, i % 2], A["ln_b_2"][i // 2, i % 2]
                pool.dma_start(LNG[:, 0, :], g.partition_broadcast(P)).then_inc(S("gains_in"), 16)
                pool.dma_start(LNG[:, 1, :], b.partition_broadcast(P)).then_inc(S("gains_in"), 16)
                if i == 0:
                    pool.dma_start(DM[:, :], A["decay"]).then_inc(S("decay_in"), 16)

        def split_low(*keys):
            for key in keys:
                n = splits[0]
                if n >= len(split_keys):
                    return
                assert split_keys[n] == key, (key, split_keys[n])
                splits[0] += 1
                r = place[key, 0][0]
                size = stream[order.index(key)][1][1] // QUARTERS
                for q in range(QUARTERS):
                    pool.wait_ge(S("hi_split"), QUARTERS * n + q + 1)
                    nc.gpsimd.tensor_tensor(WLO[:, q, 0:size], slot(r)[:, q * size:(q + 1) * size],
                                            WHI[:, q, 0:size].bitcast(F32), ALU.subtract).then_inc(S("lo_split"), 1)

        norm()
        split_low(("ckv", 0))
        norm()
        split_low(("ckv", 1), ("in", "q"), ("in", "kv"), ("in", "su"))
        norm()
        split_low(("in", "sv"), ("in", "ga0"), ("in", "ga1"))
        norm()
        split_low(("in", "gb0"), ("in", "gb1"), ("att_out", 0), ("sgu_out", 0), ("w_out", 0), ("w_out", 1))
        norm()
        split_low(("cq", 0), ("co", 0))
        norm()
        norm()
        split_low(*[("sb", j) for j in range(6)], ("sb_out", 0), ("sb_out", 1))
        norm()
        norm()
        split_low(*[("ret", j) for j in range(12)])
        for h in range(8):
            norm()
        split_low(*[("ret_out", j) for j in range(4)])
        norm()
        norm()
        pool.wait_ge(S("gains_in"), 16)
    ctx.close()


RELOADS = [7, 8, 9, 18]

NAMES = ['x', 'mem', 'g_mix', 'w_in', 'g_q', 'g_k', 'w_att_out', 'sgu_ln_g', 'sgu_ln_b', 'w_s', 'b_s', 'w_sgu_out', 'w_out',
         'g_cross', 'g_mem', 'w_cq', 'w_ckv', 'w_co', 'g_moe', 'w_rg', 'b_rg', 'w_re', 'b_re', 'w_gate', 'w_up', 'w_down',
         'g_final', 'c_2', 'positions_2', 'ada_w_2', 'ada_b_2', 'ln_g_2', 'ln_b_2', 'sb_w_in_2', 'sb_w_out_2',
         'ret_w_in_2', 'ret_gn_g_2', 'ret_w_out_2', 'router_w_2', 'router_b_2', 'moe_w_gate_2', 'moe_w_up_2', 'moe_w_down_2']
STOP = None
FINAL = {None: 5, ('co',): 1, ('moe', 0): 1, ('sb_out',): 2, ('moe', 1): 3, ('ret_out',): 4}


def kernel(**inputs):
    import concourse.bacc as bacc
    from concourse.bass_utils import run_bass_kernel_spmd

    nc = bacc.Bacc("TRN2", target_bir_lowering=False, num_devices=1)
    arrays, A = {}, {}
    given = [(name, np.ascontiguousarray(inputs[name])) for name in NAMES] + [("cst", constants()), ("decay", decay_table())]
    for name, a in given:
        arrays[f"in_{name}"] = a
        A[name] = nc.dram_tensor(f"in_{name}", a.shape, mybir.dt.from_np(a.dtype), kind="ExternalInput").ap()
    out = nc.dram_tensor("out_x", (1, SEQ, D), F32, kind="ExternalOutput").ap()
    build(nc, A, out, STOP, FINAL[STOP])
    r = run_bass_kernel_spmd(nc, [arrays], core_ids=[0])
    return r.results[0]["out_x"]
```
